# Optimizing a Trainium2 kernel written in Bass

```python
import jax, jax.numpy as jnp
from jax import lax
import numpy as np

D_MODEL = 1024
BATCH = 1
SEQ = 2048
DEPTH = 1

CHUNK = 64
N_META = 16
META_PAD = CHUNK - N_META
MIX_WIDTH = D_MODEL
SWA_WIDTH = MIX_WIDTH // 2
GLA_WIDTH = MIX_WIDTH - SWA_WIDTH
SWA_HEAD_DIM = 64
SWA_Q_HEADS = SWA_WIDTH // SWA_HEAD_DIM
SWA_KV_HEADS = 2
SWA_GROUP = SWA_Q_HEADS // SWA_KV_HEADS
WINDOW = 128
WINDOW_CHUNKS = WINDOW // CHUNK
GLA_HEADS = 4
GLA_V_DIM = GLA_WIDTH // GLA_HEADS
GLA_K_DIM = GLA_V_DIM // 2
GLA_GATE_RANK = 16
GLA_GATE_NORMALIZER = 16.0
D_FF = -(-8 * D_MODEL // (3 * 256)) * 256
RMS_EPS = 1e-6
NEG_INF = -1e30

IN_SPLITS = (
    SWA_Q_HEADS * SWA_HEAD_DIM,
    SWA_KV_HEADS * SWA_HEAD_DIM,
    SWA_KV_HEADS * SWA_HEAD_DIM,
    GLA_HEADS * GLA_K_DIM,
    GLA_HEADS * GLA_K_DIM,
    GLA_HEADS * GLA_V_DIM,
    GLA_WIDTH,
    GLA_GATE_RANK,
)
IN_WIDTH = sum(IN_SPLITS)

kernel_name = "hymba_gla_swa_sink_hybrid"

def rms_norm(x, w):
    xf = x.astype(jnp.float32)
    y = xf * lax.rsqrt(jnp.mean(xf * xf, axis=-1, keepdims=True) + RMS_EPS)
    return (y * w.astype(jnp.float32)).astype(x.dtype)

def swa_sink_attention(q, k, v, sinks, valid):
    B, L = q.shape[0], q.shape[1]
    nc = L // CHUNK
    qb = q.reshape(B, nc, CHUNK, SWA_KV_HEADS, SWA_GROUP, SWA_HEAD_DIM)
    kb = k.reshape(B, nc, CHUNK, SWA_KV_HEADS, SWA_HEAD_DIM)
    vb = v.reshape(B, nc, CHUNK, SWA_KV_HEADS, SWA_HEAD_DIM)
    vmask = valid.reshape(nc, CHUNK)
    cidx = jnp.arange(nc)
    keys = [jnp.broadcast_to(kb[:, :1], kb.shape)]
    vals = [jnp.broadcast_to(vb[:, :1], vb.shape)]
    masks = [(cidx >= WINDOW_CHUNKS)[:, None] & vmask[0][None, :]]
    for off in range(WINDOW_CHUNKS - 1, -1, -1):
        pad = ((0, 0), (off, 0), (0, 0), (0, 0), (0, 0))
        keys.append(jnp.pad(kb, pad)[:, :nc])
        vals.append(jnp.pad(vb, pad)[:, :nc])
        masks.append(jnp.pad(vmask, ((off, 0), (0, 0)))[:nc] & (cidx >= off)[:, None])
    keys = jnp.concatenate(keys, axis=2)
    vals = jnp.concatenate(vals, axis=2)
    mask = jnp.concatenate(masks, axis=1)
    scale = SWA_HEAD_DIM ** -0.5
    s = jnp.einsum('bnqhgd,bnkhd->bnhgqk', qb, keys).astype(jnp.float32) * scale
    s = jnp.where(mask[None, :, None, None, None, :], s, NEG_INF)
    sink = sinks.astype(jnp.float32).reshape(SWA_KV_HEADS, SWA_GROUP)[None, None, :, :, None]
    m = jnp.maximum(jnp.max(s, axis=-1), sink)
    p = jnp.exp(s - m[..., None])
    denom = jnp.sum(p, axis=-1) + jnp.exp(sink - m)
    p = p / denom[..., None]
    o = jnp.einsum('bnhgqk,bnkhd->bnqhgd', p.astype(vals.dtype), vals)
    return o.reshape(B, L, SWA_Q_HEADS * SWA_HEAD_DIM)

def chunk_causal_gla(q, k, v, log_a, valid):
    B, L = q.shape[0], q.shape[1]
    nc = L // CHUNK
    vm = valid[None, :, None, None]
    k = jnp.where(vm, k.astype(jnp.float32), 0.0)
    log_a = jnp.where(vm, log_a, 0.0)
    qc = q.astype(jnp.float32).reshape(B, nc, CHUNK, GLA_HEADS, GLA_K_DIM) * (GLA_K_DIM ** -0.5)
    kc = k.reshape(B, nc, CHUNK, GLA_HEADS, GLA_K_DIM)
    vc = v.astype(jnp.float32).reshape(B, nc, CHUNK, GLA_HEADS, GLA_V_DIM)
    la = log_a.reshape(B, nc, CHUNK, GLA_HEADS, GLA_K_DIM)
    cum = jnp.cumsum(la, axis=2)
    total = cum[:, :, -1]
    kdec = kc * jnp.exp(total[:, :, None] - cum)
    U = jnp.einsum('bncht,bnchv->bnhtv', kdec, vc)
    G = jnp.exp(total)

    def step(S, inp):
        g, u = inp
        S = g[..., None] * S + u
        return S, S

    S0 = jnp.zeros((B, GLA_HEADS, GLA_K_DIM, GLA_V_DIM), jnp.float32)
    _, S_all = lax.scan(step, S0, (jnp.moveaxis(G, 1, 0), jnp.moveaxis(U, 1, 0)))
    S_all = jnp.moveaxis(S_all, 0, 1)
    o = jnp.einsum('bncht,bnhtv->bnchv', qc, S_all)
    return o.reshape(B, L, GLA_HEADS, GLA_V_DIM)

def setup_inputs(seed: int = 0) -> dict:
    key = jax.random.key(seed)
    ks = jax.random.split(key, 16)
    f32 = jnp.float32
    nrm = lambda k, shape, s: jax.random.normal(k, shape, f32) * s
    return {
        "x": nrm(ks[0], (BATCH, SEQ, D_MODEL), 1.0),
        "meta_tokens": nrm(ks[1], (N_META, D_MODEL), 1.0),
        "norm1_w": 1.0 + nrm(ks[2], (DEPTH, D_MODEL), 0.01),
        "w_in": nrm(ks[3], (DEPTH, D_MODEL, IN_WIDTH), D_MODEL ** -0.5),
        "gla_gate_w2": nrm(ks[4], (DEPTH, GLA_GATE_RANK, GLA_HEADS * GLA_K_DIM), GLA_GATE_RANK ** -0.5),
        "gla_gate_b": nrm(ks[5], (DEPTH, GLA_HEADS * GLA_K_DIM), 0.1),
        "gla_norm_w": 1.0 + nrm(ks[6], (DEPTH, GLA_V_DIM), 0.01),
        "swa_sinks": nrm(ks[7], (DEPTH, SWA_Q_HEADS), 0.5),
        "w_out": nrm(ks[8], (DEPTH, MIX_WIDTH, D_MODEL), MIX_WIDTH ** -0.5),
        "norm2_w": 1.0 + nrm(ks[9], (DEPTH, D_MODEL), 0.01),
        "w_gate": nrm(ks[10], (DEPTH, D_MODEL, D_FF), D_MODEL ** -0.5),
        "w_up": nrm(ks[11], (DEPTH, D_MODEL, D_FF), D_MODEL ** -0.5),
        "w_down": nrm(ks[12], (DEPTH, D_FF, D_MODEL), D_FF ** -0.5),
        "final_norm_w": 1.0 + nrm(ks[13], (D_MODEL,), 0.01),
    }

def reference(x, meta_tokens, norm1_w, w_in, gla_gate_w2, gla_gate_b, gla_norm_w,
              swa_sinks, w_out, norm2_w, w_gate, w_up, w_down, final_norm_w):
    B = x.shape[0]
    meta = jnp.broadcast_to(meta_tokens[None].astype(x.dtype), (B, N_META, D_MODEL))
    h = jnp.concatenate([jnp.zeros((B, META_PAD, D_MODEL), x.dtype), meta, x], axis=1)
    L = h.shape[1]
    valid = jnp.arange(L) >= META_PAD
    bounds = np.cumsum(IN_SPLITS)[:-1].tolist()

    for l in range(DEPTH):
        hn = rms_norm(h, norm1_w[l])
        proj = hn @ w_in[l]
        sq, sk, sv, gq, gk, gv, gg, glr = jnp.split(proj, bounds, axis=-1)
        swa_out = swa_sink_attention(
            sq.reshape(B, L, SWA_Q_HEADS, SWA_HEAD_DIM),
            sk.reshape(B, L, SWA_KV_HEADS, SWA_HEAD_DIM),
            sv.reshape(B, L, SWA_KV_HEADS, SWA_HEAD_DIM),
            swa_sinks[l], valid)
        gate_logit = (glr @ gla_gate_w2[l] + gla_gate_b[l]).astype(jnp.float32)
        log_a = (jax.nn.log_sigmoid(gate_logit) / GLA_GATE_NORMALIZER).reshape(B, L, GLA_HEADS, GLA_K_DIM)
        gla_o = chunk_causal_gla(
            gq.reshape(B, L, GLA_HEADS, GLA_K_DIM),
            gk.reshape(B, L, GLA_HEADS, GLA_K_DIM),
            gv.reshape(B, L, GLA_HEADS, GLA_V_DIM),
            log_a, valid)
        gla_o = rms_norm(gla_o, gla_norm_w[l]).reshape(B, L, GLA_WIDTH).astype(hn.dtype)
        gla_out = gla_o * jax.nn.silu(gg)
        mix = jnp.concatenate([swa_out.astype(hn.dtype), gla_out], axis=-1) @ w_out[l]
        h = h + mix
        hn2 = rms_norm(h, norm2_w[l])
        h = h + (jax.nn.silu(hn2 @ w_gate[l]) * (hn2 @ w_up[l])) @ w_down[l]

    return rms_norm(h[:, META_PAD + N_META:], final_norm_w)


_drawn_inputs = setup_inputs


def setup_inputs(seed=0):
    import zlib

    import numpy as np

    out = dict(_drawn_inputs(seed))
    spreads = {}
    factors = {'norm1_w': 6.058,
     'gla_gate_b': 2.77,
     'gla_norm_w': 8.0,
     'swa_sinks': 8.0,
     'norm2_w': 8.0,
     'final_norm_w': 5.49}
    for name, (base, spread) in spreads.items():
        noise = np.random.default_rng([zlib.crc32(name.encode()), seed]).standard_normal(out[name].shape)
        drawn = base * np.exp(spread * noise) if base else spread * noise
        out[name] = __import__('jax').numpy.asarray(drawn.astype(out[name].dtype))
    for name, factor in factors.items():
        out[name] = (out[name] * factor).astype(out[name].dtype)
    return out
```

```python
from contextlib import ExitStack

import concourse.bass as bass
from concourse import mybir

F32 = mybir.dt.float32
F32R = mybir.dt.float32r
BF16 = mybir.dt.bfloat16
ALU = mybir.AluOpType
ACT = mybir.ActivationFunctionType
AX_X = mybir.AxisListType.X

P = 128
D = 1024
KT_N = D // P
CH = 64
META = 16
DH = 64
KEYS = CH + META + P
PREV = CH + META
QH = 8
GH = 4
DK = 64
DV = 128
BT = 4
BLK = BT * P
BLOCKS = 4
SUPER = 2
F_TILES = 22
GROUPS = F_TILES // 2
HALF = 512
UNIT = 1024
RING = 3
RANK = 16
EPS = 1e-6
SV, GK, GLR = 0, 128, 384
NARROW = 400
U_NARROW, U_Q, U_K, U_GQ, U_GV, U_GG, U_OUT = 0, 4, 8, 9, 11, 15, 19
UNITS = 27
FFN_UNITS = 6 * GROUPS
C_ID, C_TRI, C_CHUNK, CONSTS = 0, 128, 256, 258
M_ROW, M_MASK, M_MASK0, MASKS = 0, 128, 336, 544


def quarter(b, u, c):
    return 4 * (UNITS * b + u) + c + 1


def build(nc, x, meta, n1w, n2w, fw, w_block, w_ffn, w2b, gw, sinks, consts, masks, h_mid, out):
    with ExitStack() as outer:
        def alloc(stack, name, shape, dt=F32):
            return stack.enter_context(nc.sbuf_tensor(name, shape, dt))

        def sem(name):
            return outer.enter_context(nc.semaphore(name))

        stage = [alloc(outer, f"stage{i}", [P, UNIT]) for i in range(RING)]
        w_hi = [alloc(outer, f"w_hi{i}", [P, UNIT], F32R) for i in range(RING)]
        w_lo = [alloc(outer, f"w_lo{i}", [P, UNIT], F32R) for i in range(RING)]
        cst = alloc(outer, "cst", [P, CONSTS])
        n1 = alloc(outer, "n1", [P, KT_N])
        n2 = alloc(outer, "n2", [P, KT_N])
        junk = alloc(outer, "junk", [P, D], BF16)
        neg_half = alloc(outer, "neg_half", [P, GH * BT])
        dense = outer.enter_context(nc.psum_tensor("dense", [P, 4, HALF], F32))
        aux = outer.enter_context(nc.psum_tensor("aux", [P, 4, HALF], F32))
        ident = cst[:, C_ID:C_ID + P]
        tri = cst[:, C_TRI:C_TRI + P]

        c_in = sem("c_in")

        def wait_alone(eng, *waits):
            for _, value in waits:
                eng.compute_val(value)
            eng.wait_ge(c_in, 16 * 7)
            for signal, value in waits:
                eng.wait_ge(signal, value)

        w_loaded = [sem(f"w_loaded{i}") for i in range(RING)]
        w_hi_ready = sem("w_hi_ready")
        w_lo_ready = sem("w_lo_ready")
        dense_done = sem("dense_done")
        ffn_done = sem("ffn_done")

        def load_unit(sp, slot, src):
            sp.dma_start(stage[slot][:], src).then_inc(w_loaded[slot], 16)

        def split_hi(act, n, slot, round_):
            act.wait_ge(w_loaded[slot], 16 * (round_ + 1))
            nc.scalar.activation(w_hi[slot][:], stage[slot][:], ACT.Copy).then_inc(w_hi_ready, 1)

        def split_lo(dve, n, slot):
            dve.wait_ge(w_hi_ready, n + 1)
            nc.vector.tensor_tensor(w_lo[slot][:], stage[slot][:], w_hi[slot][:].bitcast(F32),
                                    ALU.subtract).then_inc(w_lo_ready, 1)

        def three_pass(out_ap, a_hi, a_lo, b_hi, b_lo, first, last):
            nc.tensor.matmul(out_ap, a_hi, b_lo, start=first, stop=False)
            nc.tensor.matmul(out_ap, a_lo, b_hi, start=False, stop=False)
            return nc.tensor.matmul(out_ap, a_hi, b_hi, start=False, stop=last)

        x_in = sem("x_in")
        ss1_ready = sem("ss1_ready")
        ms1_ready = sem("ms1_ready")
        rstd1_ready = sem("rstd1_ready")
        xn_ready = sem("xn_ready")
        xt_ready = sem("xt_ready")
        xt_hi = sem("xt_hi")
        xt_lo = sem("xt_lo")
        xr_in = sem("xr_in")
        h_stored = sem("h_stored")

        mixer = outer.enter_context(ExitStack())
        xn = alloc(mixer, "xn", [P, BT, D])
        hn_hi = alloc(mixer, "hn_hi", [P, KT_N, BLK], F32R)
        hn_lo = alloc(mixer, "hn_lo", [P, KT_N, BLK], F32R)
        ss1 = alloc(mixer, "ss1", [P, BT])
        ms1 = alloc(mixer, "ms1", [P, BT])
        rstd1 = alloc(mixer, "rstd1", [P, BT])
        keys = alloc(mixer, "keys", [P, BT + 1, KEYS])
        v_prev = alloc(mixer, "v_prev", [PREV, BT + 1, P])
        state = alloc(mixer, "state", [P, 2 * BT, 2, DV])
        w2 = alloc(mixer, "w2", [RANK + 1, GH * DK])
        row_ind = alloc(mixer, "row_ind", [P, P], BF16)
        mask = alloc(mixer, "mask", [P, 2, KEYS], BF16)
        nsink = alloc(mixer, "nsink", [P, QH])
        sinkb = alloc(mixer, "sinkb", [P, QH])
        sinki = alloc(mixer, "sinki", [P, QH])
        gwb = alloc(mixer, "gwb", [P, DV])

        def load_x(eng, b):
            eng.dma_start(xn[:], x[b]).then_inc(x_in, 16)

        def norm1_squares(act, b):
            act.wait_ge(x_in, 16 * (b + 1))
            for t in range(BT):
                if t > 0:
                    act.wait_ge(ss1_ready, BT * b + t)
                nc.scalar.activation(junk[:], xn[:, t, :], ACT.Square,
                                     accum_out=ss1[:, t:t + 1]).then_inc(ss1_ready, 1)

        def norm1_rstd(pool, b):
            pool.wait_ge(ms1_ready, b + 1)
            nc.gpsimd.tensor_tensor(rstd1[:], ms1[:], neg_half[:, 0:BT], ALU.pow).then_inc(rstd1_ready, 1)

        def norm1_mean(dve, b):
            dve.wait_ge(ss1_ready, BT * b + BT)
            nc.vector.tensor_scalar(ms1[:], ss1[:], 1.0 / D, EPS, ALU.mult, ALU.add).then_inc(ms1_ready, 1)

        def norm1_scale(dve, b):
            dve.wait_ge(rstd1_ready, b + 1)
            for t in range(BT):
                nc.vector.tensor_scalar(xn[:, t, :], xn[:, t, :], rstd1[:, t:t + 1], None,
                                        ALU.mult).then_inc(xn_ready, 1)

        def norm1_transpose(pe, b, k):
            for t in range(BT):
                last = nc.tensor.transpose(aux[:, k % 4, t * P:(t + 1) * P], xn[:, t, k * P:(k + 1) * P], ident)
            last.then_inc(xt_ready, 1)

        def norm1_hi(act, b, k):
            act.wait_ge(xt_ready, KT_N * b + k + 1)
            nc.scalar.activation(hn_hi[:, k, :], aux[:, k % 4, :], ACT.Copy,
                                 scale=n1[:, k:k + 1]).then_inc(xt_hi, 1)

        def norm1_lo(dve, b, k):
            dve.wait_ge(xt_hi, KT_N * b + k + 1)
            nc.vector.scalar_tensor_tensor(out=hn_lo[:, k, :], in0=aux[:, k % 4, :], scalar=n1[:, k:k + 1],
                                           in1=hn_hi[:, k, :].bitcast(F32), op0=ALU.mult,
                                           op1=ALU.subtract).then_inc(xt_lo, 1)

        with ExitStack() as st:
            WK, WN, WV = 0, 1, 5
            wm = alloc(st, "wm", [P, 9, UNIT])
            mx = alloc(st, "mx", [META, D])
            masks_in = alloc(st, "masks_in", [P, MASKS])
            mss = alloc(st, "mss", [META, 1])
            mms = alloc(st, "mms", [META, 1])
            mrs = alloc(st, "mrs", [META, 1])
            mt = alloc(st, "mt", [P, KT_N, META])
            mn = alloc(st, "mn", [META, NARROW])
            mv = alloc(st, "mv", [META, GH * DV])
            mg = alloc(st, "mg", [RANK + 1, META])
            ga = alloc(st, "ga", [META, GH * DK])
            gb = alloc(st, "gb", [META, GH * DK])
            m_in = sem("m_in")
            mw_in = sem("mw_in")
            m_act = sem("m_act")
            m_dve = sem("m_dve")
            m_pool = sem("m_pool")
            m_pe = sem("m_pe")
            with nc.Block() as block:
                @block.sync
                def _(sp):
                    sp.dma_start(mx[:], meta).then_inc(m_in, 16)
                    for dst, src in ((cst, consts), (masks_in, masks), (n1, n1w), (n2, n2w), (w2, w2b), (gwb, gw), (sinki, sinks)):
                        sp.dma_start(dst[:], src).then_inc(c_in, 16)
                    sp.dma_start(wm[:, WK, :], w_block[U_K]).then_inc(mw_in, 16)
                    for i in range(4):
                        sp.dma_start(wm[:, WN + i, :], w_block[U_NARROW + i]).then_inc(mw_in, 16)
                    for i in range(4):
                        sp.dma_start(wm[:, WV + i, :], w_block[U_GV + i]).then_inc(mw_in, 16)
                    load_x(sp, 0)
                    for u in range(RING):
                        load_unit(sp, u, w_block[u])

                @block.scalar
                def _(act):
                    nc.scalar.preload_act_table_set("natural_log_exp_and_others")
                    act.wait_ge(m_in, 16)
                    nc.scalar.activation(junk[0:META, :], mx[:], ACT.Square, accum_out=mss[:]).then_inc(m_act, 1)
                    act.wait_ge(m_pe, 4)
                    nc.scalar.activation(ga[:], aux[0:META, 1, 0:GH * DK], ACT.Abs).then_inc(m_act, 1)
                    act.wait_ge(m_act, 2)
                    nc.scalar.activation(gb[:], ga[:], ACT.Exp, scale=-1.0).then_inc(m_act, 1)
                    act.wait_ge(m_act, 3)
                    nc.scalar.activation(ga[:], gb[:], ACT.Ln, bias=1.0).then_inc(m_act, 1)
                    act.wait_ge(m_pe, 5)
                    nc.scalar.activation(ga[:], aux[0:META, 2, 0:GH * DK], ACT.Exp).then_inc(m_act, 1)
                    norm1_squares(act, 0)
                    for k in range(KT_N):
                        norm1_hi(act, 0, k)
                    for u in range(RING):
                        split_hi(act, u, u, 0)

                @block.gpsimd
                def _(pool):
                    nc.gpsimd.memset(neg_half[:], -0.5).then_inc(m_pool, 1)
                    pool.wait_ge(m_act, 1)
                    nc.gpsimd.tensor_scalar(mms[:], mss[:], 1.0 / D, EPS, ALU.mult, ALU.add).then_inc(m_pool, 1)
                    pool.wait_ge(m_pool, 2)
                    nc.gpsimd.tensor_tensor(mrs[:], mms[:], neg_half[0:META, 0:1], ALU.pow).then_inc(m_pool, 1)
                    norm1_rstd(pool, 0)

                @block.vector
                def _(dve):
                    nc.vector.memset(mg[:], 1.0)
                    nc.vector.memset(keys[:, BT, 0:CH], 0.0)
                    nc.vector.memset(v_prev[0:CH, BT, :], 0.0).then_inc(m_dve, 1)
                    dve.wait_ge(c_in, 16 * 7)
                    nc.vector.tensor_copy(row_ind[:], masks_in[:, M_ROW:M_ROW + P])
                    nc.vector.tensor_copy(mask[:, 0, :], masks_in[:, M_MASK0:M_MASK0 + KEYS])
                    nc.vector.tensor_copy(mask[:, 1, :], masks_in[:, M_MASK:M_MASK + KEYS])
                    nc.vector.tensor_copy(sinkb[:].rearrange("p (s g j) -> p s g j", s=2, g=2),
                                          sinki[:].rearrange("p (g s j) -> p s g j", s=2, g=2)).then_inc(m_dve, 1)
                    dve.wait_ge(m_dve, 2)
                    nc.vector.tensor_scalar(nsink[:], sinkb[:], -1.0, None, ALU.mult).then_inc(m_dve, 1)
                    dve.wait_ge(m_pool, 3)
                    nc.vector.tensor_scalar(mx[:], mx[:], mrs[:], None, ALU.mult).then_inc(m_dve, 1)
                    dve.wait_ge(m_pe, 1)
                    nc.vector.tensor_tensor(mt[:], aux[:, 0, 0:KT_N * META].rearrange("p (k m) -> p k m", k=KT_N),
                                            n1[:].unsqueeze(2).to_broadcast([P, KT_N, META]),
                                            ALU.mult).then_inc(m_dve, 1)
                    dve.wait_ge(m_pe, 2)
                    for t in range(BT + 1):
                        nc.vector.tensor_copy(keys[:, t, CH:PREV], aux[:, 1, 0:META])
                        nc.vector.tensor_copy(v_prev[CH:PREV, t, :], aux[0:META, 2, SV:SV + P])
                    nc.vector.tensor_copy(mn[:], aux[0:META, 2, 0:NARROW])
                    nc.vector.tensor_copy(mv[:], aux[0:META, 3, :]).then_inc(m_dve, 1)
                    dve.wait_ge(m_pe, 3)
                    nc.vector.tensor_copy(mg[0:RANK, :], aux[0:RANK, 0, 0:META]).then_inc(m_dve, 1)
                    dve.wait_ge(m_act, 4)
                    nc.vector.scalar_tensor_tensor(out=gb[:], in0=aux[0:META, 1, 0:GH * DK], scalar=0.0,
                                                   in1=ga[:], op0=ALU.min, op1=ALU.subtract).then_inc(m_dve, 1)
                    dve.wait_ge(m_act, 5)
                    nc.vector.tensor_tensor(gb[:], mn[:, GK:GK + GH * DK], ga[:], ALU.mult).then_inc(m_dve, 1)
                    dve.wait_ge(m_pe, 6)
                    nc.vector.tensor_copy(state[:, 2 * BT - 1, :, :],
                                          aux[:, 3, 0:2 * DV].rearrange("p (a v) -> p a v", a=2)).then_inc(m_dve, 1)
                    norm1_mean(dve, 0)
                    norm1_scale(dve, 0)
                    for k in range(KT_N):
                        norm1_lo(dve, 0, k)
                    for u in range(RING):
                        split_lo(dve, u, u)

                @block.tensor
                def _(pe):
                    pe.wait_ge(c_in, 16 * 7)
                    pe.wait_ge(m_dve, 4)
                    for k in range(KT_N):
                        last = nc.tensor.transpose(aux[:, 0, k * META:(k + 1) * META], mx[:, k * P:(k + 1) * P],
                                                   ident[0:META, 0:META])
                    last.then_inc(m_pe, 1)
                    pe.wait_ge(m_dve, 5)
                    pe.wait_ge(mw_in, 16 * 9)
                    for k in range(KT_N):
                        nc.tensor.matmul(aux[:, 1, 0:META], wm[:, WK, k * P:(k + 1) * P], mt[:, k, :],
                                         start=k == 0, stop=k == KT_N - 1)
                    for k in range(KT_N):
                        nc.tensor.matmul(aux[0:META, 2, 0:NARROW], mt[:, k, :],
                                         wm[:, WN + k // 2, (k % 2) * HALF:(k % 2) * HALF + NARROW],
                                         start=k == 0, stop=k == KT_N - 1)
                    for k in range(KT_N):
                        last = nc.tensor.matmul(aux[0:META, 3, :], mt[:, k, :],
                                                wm[:, WV + k // 2, (k % 2) * HALF:(k % 2 + 1) * HALF],
                                                start=k == 0, stop=k == KT_N - 1)
                    last.then_inc(m_pe, 1)
                    pe.wait_ge(m_dve, 6)
                    nc.tensor.transpose(aux[0:RANK, 0, 0:META], mn[:, GLR:GLR + RANK],
                                        ident[0:META, 0:META]).then_inc(m_pe, 1)
                    pe.wait_ge(m_dve, 7)
                    nc.tensor.matmul(aux[0:META, 1, 0:GH * DK], mg[:], w2[:], start=True, stop=True).then_inc(m_pe, 1)
                    pe.wait_ge(m_dve, 8)
                    nc.tensor.matmul(aux[0:META, 2, 0:GH * DK], tri[0:META, 0:META], gb[:],
                                     start=True, stop=True).then_inc(m_pe, 1)
                    pe.wait_ge(m_dve, 9)
                    for h in range(GH):
                        last = nc.tensor.matmul(aux[(h % 2) * DK:(h % 2 + 1) * DK, 3, (h // 2) * DV:(h // 2 + 1) * DV],
                                                gb[:, h * DK:(h + 1) * DK], mv[:, h * DV:(h + 1) * DV],
                                                start=True, stop=True)
                    last.then_inc(m_pe, 1)
                    pe.wait_ge(m_dve, 10)
                    pe.wait_ge(xn_ready, BT)
                    for k in range(KT_N):
                        if k >= 4:
                            pe.wait_ge(xt_lo, k - 3)
                        norm1_transpose(pe, 0, k)

        mx_st = mixer.enter_context(ExitStack())
        xr = alloc(mx_st, "xr", [P, BT, HALF])
        mix_hi = alloc(mx_st, "mix_hi", [P, KT_N, BLK], F32R)
        mix_lo = alloc(mx_st, "mix_lo", [P, KT_N, BLK], F32R)
        mix_swa = alloc(mx_st, "mix_swa", [P, BT, QH * DH])
        q_sb = alloc(mx_st, "q_sb", [P, 4, BLK])
        gq_sb = alloc(mx_st, "gq_sb", [P, 2, BLK])
        narrow = alloc(mx_st, "narrow", [P, BT, NARROW])
        gv_sb = alloc(mx_st, "gv_sb", [P, BT, GH * DV])
        sg = alloc(mx_st, "sg", [P, BT, GH * DV])
        gate_a = alloc(mx_st, "gate_a", [P, BT * GH * DK])
        gate_b = alloc(mx_st, "gate_b", [P, BT * GH * DK])
        rank_t = alloc(mx_st, "rank_t", [RANK + 1, BLK])
        chunk_g = alloc(mx_st, "chunk_g", [P, 4 * BT])
        gss = alloc(mx_st, "gss", [P, GH * BT])
        gms = alloc(mx_st, "gms", [P, GH * BT])
        grs = alloc(mx_st, "grs", [P, GH * BT])
        probs = alloc(mx_st, "probs", [P, 4, KEYS])
        pt_own = alloc(mx_st, "pt_own", [P, 4, P])
        pt_prev = alloc(mx_st, "pt_prev", [PREV, 4, P])
        smax = alloc(mx_st, "smax", [P, 2, 4])
        nmax = alloc(mx_st, "nmax", [P, 2, 4])
        esink_in = alloc(mx_st, "esink_in", [P, 2, 4])
        esink = alloc(mx_st, "esink", [P, 2, 4])
        rowsum = alloc(mx_st, "rowsum", [P, 2, 4])
        denom = alloc(mx_st, "denom", [P, 2, 4])
        rden = alloc(mx_st, "rden", [P, 2, 4])

        rank_ready = sem("rank_ready")
        logit_ready = sem("logit_ready")
        decay_ready = sem("decay_ready")
        scores_ready = sem("scores_ready")
        pt_ready = sem("pt_ready")
        pv_ready = sem("pv_ready")
        u_ready = sem("u_ready")
        o_ready = sem("o_ready")
        mt_ready = sem("mt_ready")
        q_out = sem("q_out")
        gq_out = sem("gq_out")
        gv_out = sem("gv_out")
        rank_out = sem("rank_out")
        gate_act = sem("gate_act")
        decay_exp = sem("decay_exp")
        exp_done = sem("exp_done")
        pt_own_out = sem("pt_own_out")
        o_out_act = sem("o_out_act")
        sq_ready = sem("sq_ready")
        gg_out = sem("gg_out")
        mt_hi = sem("mt_hi")
        carried = sem("carried")
        narrow_out = sem("narrow_out")
        k_out = sem("k_out")
        la_ready = sem("la_ready")
        kdec_ready = sem("kdec_ready")
        smax_ready = sem("smax_ready")
        nmax_ready = sem("nmax_ready")
        denom_ready = sem("denom_ready")
        pt_prev_out = sem("pt_prev_out")
        swa_out = sem("swa_out")
        state_ready = sem("state_ready")
        o_out_dve = sem("o_out_dve")
        gss_ready = sem("gss_ready")
        gms_ready = sem("gms_ready")
        gla_scaled = sem("gla_scaled")
        gla_out = sem("gla_out")
        mt_lo = sem("mt_lo")
        res_added = sem("res_added")
        grs_ready = sem("grs_ready")
        sgw_ready = sem("sgw_ready")

        def next_unit(b, u, last):
            v = u + RING
            if v < UNITS:
                return w_block[v]
            return w_ffn[v - UNITS] if last else w_block[v - UNITS]

        def p1_retire_load(sp, b, u, last):
            sp.wait_ge(w_lo_ready, UNITS * b + u + 1)
            load_unit(sp, u % RING, next_unit(b, u, last))

        def p1_retire_hi(act, b, u):
            act.wait_ge(dense_done, quarter(b, u, 3))
            split_hi(act, UNITS * b + u + RING, u % RING, (UNITS // RING) * b + u // RING + 1)

        def p1_retire_lo(dve, b, u):
            split_lo(dve, UNITS * b + u + RING, u % RING)

        def load_xr(sp, b, half):
            sp.dma_start(xr[:], x[b][:, :, half * HALF:(half + 1) * HALF]).then_inc(xr_in, 16)

        def store_h(sp, b, half):
            sp.wait_ge(res_added, 8 * b + 4 * half + 4)
            sp.dma_start(h_mid[2 * b + half], xr[:].rearrange("p t n -> p (t n)")).then_inc(h_stored, 16)
            sp.wait_ge(h_stored, 16 * (2 * b + half + 1))

        def sp_block(sp, b, last):
            for u in range(RING, UNITS):
                p1_retire_load(sp, b, u, last)
                if u == U_K and not last:
                    sp.wait_ge(xt_ready, KT_N * b + KT_N)
                    load_x(sp, b + 1)
                if u == UNITS - 2:
                    store_h(sp, b, 0)
                    load_xr(sp, b, 1)
            if not last:
                for u in range(RING):
                    p1_retire_load(sp, b + 1, u, last)
            store_h(sp, b, 1)
            if not last:
                load_xr(sp, b + 1, 0)

        def pe_block(pe, b, last):
            def unit(u):
                pe.wait_ge(w_lo_ready, UNITS * b + u + 1)

            def feature_quarter(u, bank, c):
                s = u % RING
                for k in (2 * c, 2 * c + 1):
                    w = slice(k * P, (k + 1) * P)
                    ins = three_pass(dense[:, bank, :], w_hi[s][:, w], w_lo[s][:, w],
                                     hn_hi[:, k, :], hn_lo[:, k, :], k == 0, k == KT_N - 1)
                ins.then_inc(dense_done, 1)

            def token_quarter(u, q, t, a_hi, a_lo, cols):
                s = u % RING
                for i in range(2):
                    k = 2 * q + i
                    w = slice(i * HALF, i * HALF + cols)
                    ins = three_pass(dense[:, t, 0:cols], a_hi[:, k, t * P:(t + 1) * P],
                                     a_lo[:, k, t * P:(t + 1) * P], w_hi[s][:, w], w_lo[s][:, w],
                                     k == 0, k == KT_N - 1)
                ins.then_inc(dense_done, 1)

            for q in range(4):
                unit(U_NARROW + q)
                pe.wait_ge(xt_lo, KT_N * b + 2 * q + 2)
                for t in range(BT):
                    if q == 0 and t == 0:
                        pe.wait_ge(carried, b + 1)
                    token_quarter(U_NARROW + q, q, t, hn_hi, hn_lo, NARROW)

            def rank_transposes():
                pe.wait_ge(narrow_out, BT * b + BT)
                for t in range(BT):
                    ins = nc.tensor.transpose(aux[0:RANK, 0, t * P:(t + 1) * P],
                                              narrow[:, t, GLR:GLR + RANK], ident)
                ins.then_inc(rank_ready, 1)

            def logits():
                pe.wait_ge(rank_out, b + 1)
                for t in range(BT):
                    ins = nc.tensor.matmul(aux[:, 2 + t // 2, (t % 2) * 256:(t % 2 + 1) * 256],
                                           rank_t[:, t * P:(t + 1) * P], w2[:], start=True, stop=True)
                ins.then_inc(logit_ready, 1)

            def decays():
                pe.wait_ge(la_ready, b + 1)
                for i in range(2):
                    nc.tensor.matmul(aux[:, i, :], tri, gate_b[:, i * HALF:(i + 1) * HALF], start=True, stop=True)
                for t in range(BT):
                    for p in range(2):
                        c = t * 4 + p * 2
                        ins = nc.tensor.matmul(aux[:, 2, c:c + 2], gate_b[:, t * 256 + p * P:t * 256 + (p + 1) * P],
                                               cst[:, C_CHUNK:C_CHUNK + 2], start=True, stop=True)
                ins.then_inc(decay_ready, 1)

            for j in range(5):
                unit(U_Q + j)
                if j < 4:
                    pe.wait_ge(narrow_out, BT * b + j + 1)
                else:
                    pe.wait_ge(q_out, 4 * b + 1)
                for c in range(4):
                    feature_quarter(U_Q + j, j % 4, c)
                if j == 0:
                    rank_transposes()
                if j == 1:
                    logits()
                if j == 3:
                    decays()

            def scores(s):
                t, hs = divmod(s, 2)
                if s == 0:
                    pe.wait_ge(q_out, 4 * b + 4)
                    pe.wait_ge(k_out, b + 1)
                    pe.wait_ge(decay_exp, 2 * b + 2)
                else:
                    pe.wait_ge(exp_done, 8 * b + s)
                for g in range(2):
                    r = slice(g * DH, (g + 1) * DH)
                    for j in range(2):
                        o = aux[:, g, j * KEYS:(j + 1) * KEYS]
                        nc.tensor.matmul(o, row_ind[r, :], mask[r, 0 if t == 0 else 1, :], start=True, stop=False)
                        ins = nc.tensor.matmul(o, q_sb[r, 2 * hs + j, t * P:(t + 1) * P], keys[r, t, :],
                                               start=False, stop=True)
                ins.then_inc(scores_ready, 1)

            def prob_transposes(s):
                pe.wait_ge(exp_done, 8 * b + s + 1)
                if s > 0:
                    pe.wait_ge(swa_out, 8 * b + s)
                for i in range(4):
                    nc.tensor.transpose(aux[:, 2, i * P:(i + 1) * P], probs[:, i, PREV:KEYS], ident)
                for i in range(4):
                    ins = nc.tensor.transpose(aux[0:PREV, 3, i * P:(i + 1) * P], probs[:, i, 0:PREV], ident)
                ins.then_inc(pt_ready, 1)

            def weighted_values(s):
                t = s // 2
                pe.wait_ge(pt_own_out, 8 * b + s + 1)
                pe.wait_ge(pt_prev_out, 8 * b + s + 1)
                for i in range(4):
                    v = slice((i // 2) * DH, (i // 2 + 1) * DH)
                    nc.tensor.matmul(aux[:, 2, i * DH:(i + 1) * DH], pt_prev[:, i, :], v_prev[:, t, v],
                                     start=True, stop=False)
                    ins = nc.tensor.matmul(aux[:, 2, i * DH:(i + 1) * DH], pt_own[:, i, :], narrow[:, t, v],
                                           start=False, stop=True)
                ins.then_inc(pv_ready, 1)

            def gla_in_piece(c):
                u, r = U_GQ + c // 4, c % 4
                if r == 0:
                    unit(u)
                if u < U_GV:
                    bank = 1 + u - U_GQ
                    if r == 0:
                        pe.wait_ge(q_out, 4 * b + bank + 1)
                    feature_quarter(u, bank, r)
                else:
                    if u == U_GV and r == 0:
                        pe.wait_ge(k_out, b + 1)
                    elif u == U_GV and r < 3:
                        pe.wait_ge(gq_out, 2 * b + r)
                    token_quarter(u, u - U_GV, r, hn_hi, hn_lo, HALF)

            def gg_piece(q, t):
                if t == 0:
                    unit(U_GG + q)
                if q == 0:
                    pe.wait_ge(gv_out, BT * b + t + 1)
                token_quarter(U_GG + q, q, t, hn_hi, hn_lo, HALF)

            scores(0)
            for c in range(3):
                gla_in_piece(c)
            for s in range(7):
                prob_transposes(s)
                scores(s + 1)
                gla_in_piece(3 + 3 * s)
                weighted_values(s)
                gla_in_piece(4 + 3 * s)
                gla_in_piece(5 + 3 * s)
            prob_transposes(7)
            gg_piece(0, 0)
            weighted_values(7)
            for t in range(1, 4):
                gg_piece(0, t)

            wait_alone(pe, (kdec_ready, b + 1), (gv_out, BT * b + BT), (exp_done, 8 * b + 8), (swa_out, 8 * b + 8))
            for c in range(2 * BT):
                t, i = divmod(c, 2)
                r = slice(i * CH, (i + 1) * CH)
                for h in range(GH):
                    j, p = h % 2, h // 2
                    o = (t % 2) * 256 + p * DV
                    ins = nc.tensor.matmul(
                        aux[j * DK:(j + 1) * DK, 2 * i + t // 2, o:o + DV],
                        gate_b[r, t * 256 + h * DK:t * 256 + (h + 1) * DK], gv_sb[r, t, h * DV:(h + 1) * DV],
                        start=True, stop=True)
                if c % 4 == 3:
                    ins.then_inc(u_ready, 1)
            for t in range(BT):
                gg_piece(1, t)

            def gla_read(hf):
                wait_alone(pe, (state_ready, 16 * b + 8 * hf + 8), (gq_out, 2 * b + 2))
                for c in range(4 * hf, 4 * hf + 4):
                    t, i = divmod(c, 2)
                    for h in range(GH):
                        j, p = h % 2, h // 2
                        r = slice(j * DK, (j + 1) * DK)
                        o = (t % 2) * 256 + p * DV
                        ins = nc.tensor.matmul(aux[i * CH:(i + 1) * CH, 2 * j + hf, o:o + DV],
                                               gq_sb[r, p, c * CH:(c + 1) * CH], state[r, c, p, :],
                                               start=True, stop=True)
                ins.then_inc(o_ready, 1)

            gla_read(0)
            for t in range(BT):
                gg_piece(2, t)
            gla_read(1)

            def mix_transposes(k):
                if k < 4:
                    pe.wait_ge(o_out_act, 2 * b + 2)
                    pe.wait_ge(o_out_dve, 2 * b + 2)
                else:
                    pe.wait_ge(gla_out, 2 * b + 2)
                    pe.wait_ge(mt_lo, KT_N * b + k - 3)
                src = mix_swa if k < 4 else gv_sb
                for t in range(BT):
                    ins = nc.tensor.transpose(aux[:, k % 4, t * P:(t + 1) * P],
                                              src[:, t, (k % 4) * P:(k % 4 + 1) * P], ident)
                ins.then_inc(mt_ready, 1)

            def out_unit(half, q):
                u = U_OUT + 4 * half + q
                unit(u)
                pe.wait_ge(mt_lo, KT_N * b + 2 * q + 2)
                for t in range(BT):
                    if q == 0 and half == 0:
                        pe.wait_ge(gg_out, BT * b + t + 1)
                    if q == 0 and half == 1:
                        pe.wait_ge(res_added, 8 * b + t + 1)
                    token_quarter(u, q, t, mix_hi, mix_lo, HALF)

            def next_norm(k0):
                for k in range(k0, k0 + 4):
                    if k < 4:
                        pe.wait_ge(xn_ready, BT * (b + 1) + BT)
                        pe.wait_ge(mt_lo, KT_N * b + 5 + k)
                    else:
                        pe.wait_ge(xt_lo, KT_N * (b + 1) + k - 3)
                    norm1_transpose(pe, b + 1, k)

            gg_piece(3, 0)
            gg_piece(3, 1)
            for k in range(4):
                mix_transposes(k)
            gg_piece(3, 2)
            gg_piece(3, 3)
            out_unit(0, 0)
            out_unit(0, 1)
            for k in range(4, 8):
                mix_transposes(k)
            out_unit(0, 2)
            out_unit(0, 3)
            out_unit(1, 0)
            if not last:
                next_norm(0)
            out_unit(1, 1)
            out_unit(1, 2)
            if not last:
                next_norm(4)
            out_unit(1, 3)

        def act_block(act, b, last):
            def retire(u):
                p1_retire_hi(act, b, u)

            def q_evacuate(j):
                act.wait_ge(dense_done, quarter(b, U_Q + j, 3))
                nc.scalar.activation(q_sb[:, j, :], dense[:, j, :], ACT.Copy).then_inc(q_out, 1)

            for u in range(4):
                retire(u)
            q_evacuate(0)
            retire(4)
            act.wait_ge(rank_ready, b + 1)
            nc.scalar.activation(rank_t[0:RANK, :], aux[0:RANK, 0, :], ACT.Copy).then_inc(rank_out, 1)
            q_evacuate(1)
            retire(5)
            act.wait_ge(logit_ready, b + 1)
            nc.scalar.activation(gate_a[:].rearrange("p (a n) -> p a n", a=2), aux[:, 2:4, :],
                                 ACT.Abs).then_inc(gate_act, 1)
            act.wait_ge(gate_act, 3 * b + 1)
            nc.scalar.activation(gate_a[:], gate_a[:], ACT.Exp, scale=-1.0).then_inc(gate_act, 1)
            act.wait_ge(gate_act, 3 * b + 2)
            nc.scalar.activation(gate_a[:], gate_a[:], ACT.Ln, bias=1.0).then_inc(gate_act, 1)
            q_evacuate(2)
            retire(6)
            q_evacuate(3)
            retire(7)
            act.wait_ge(decay_ready, b + 1)
            nc.scalar.activation(gate_a[:].rearrange("p (a n) -> p a n", a=2), aux[:, 0:2, :],
                                 ACT.Exp).then_inc(decay_exp, 1)
            nc.scalar.activation(chunk_g[:], aux[:, 2, 0:4 * BT], ACT.Exp).then_inc(decay_exp, 1)
            retire(8)

            def exps(s):
                act.wait_ge(nmax_ready, 16 * b + 2 * s + 2)
                r = s % 2
                nc.scalar.activation(esink[:, r, :], esink_in[:, r, :], ACT.Exp)
                for i in range(4):
                    ins = nc.scalar.activation(probs[:, i, :], aux[:, i // 2, (i % 2) * KEYS:(i % 2 + 1) * KEYS],
                                               ACT.Exp, bias=nmax[:, r, i:i + 1], scale=DH ** -0.5,
                                               accum_out=rowsum[:, r, i:i + 1])
                ins.then_inc(exp_done, 1)

            exps(0)
            for s in range(8):
                act.wait_ge(pt_ready, 8 * b + s + 1)
                nc.scalar.activation(pt_own[:].rearrange("p i q -> p (i q)"), aux[:, 2, :],
                                     ACT.Copy).then_inc(pt_own_out, 1)
                if s < 7:
                    exps(s + 1)
                for c in range(3 + 3 * s, 6 + 3 * s):
                    if c >= 24:
                        break
                    if c in (3, 7):
                        i = c // 4
                        act.wait_ge(dense_done, quarter(b, U_GQ + i, 3))
                        nc.scalar.activation(gq_sb[:, i, :], dense[:, 1 + i, :], ACT.Copy,
                                             scale=DK ** -0.5).then_inc(gq_out, 1)
                    if c >= 20:
                        t = c - 20
                        act.wait_ge(dense_done, quarter(b, U_GV + 3, t))
                        nc.scalar.activation(gv_sb[:, t, :], dense[:, t, :], ACT.Copy).then_inc(gv_out, 1)
                    if c % 4 == 3:
                        retire(U_GQ + c // 4)
            nc.scalar.preload_act_table_set("silu_and_others")
            retire(U_GG)

            def o_evacuate(hf):
                act.wait_ge(o_ready, 2 * b + hf + 1)
                nc.scalar.activation(
                    gv_sb[:, 2 * hf:2 * hf + 2, :].rearrange("p t (a j v) -> p t a j v", a=2, j=2)[:, :, :, 0, :],
                    aux[:, hf, :].rearrange("p (t a v) -> p t a v", t=2, a=2), ACT.Copy).then_inc(o_out_act, 1)
                act.wait_ge(o_out_act, 2 * b + hf + 1)
                act.wait_ge(o_out_dve, 2 * b + hf + 1)
                nc.scalar.activation(q_sb[:, 2 * hf:2 * hf + 2, :], gv_sb[:, 2 * hf:2 * hf + 2, :],
                                     ACT.Square).then_inc(sq_ready, 1)

            retire(U_GG + 1)
            o_evacuate(0)
            retire(U_GG + 2)
            o_evacuate(1)

            def mix_evacuate(k):
                act.wait_ge(mt_ready, KT_N * b + k + 1)
                nc.scalar.activation(mix_hi[:, k, :], aux[:, k % 4, :], ACT.Copy).then_inc(mt_hi, 1)

            def gg_silu(t):
                act.wait_ge(dense_done, quarter(b, U_GG + 3, t))
                nc.scalar.activation(sg[:, t, :], dense[:, t, :], ACT.Silu).then_inc(gg_out, 1)

            gg_silu(0)
            gg_silu(1)
            for k in range(4):
                mix_evacuate(k)
            gg_silu(2)
            gg_silu(3)
            retire(U_GG + 3)
            retire(U_OUT)
            if not last:
                norm1_squares(act, b + 1)
            retire(U_OUT + 1)
            for k in range(4, 8):
                mix_evacuate(k)
            retire(U_OUT + 2)
            retire(U_OUT + 3)
            retire(U_OUT + 4)
            if not last:
                for k in range(4):
                    norm1_hi(act, b + 1, k)
            retire(U_OUT + 5)
            retire(U_OUT + 6)
            if not last:
                for k in range(4, 8):
                    norm1_hi(act, b + 1, k)
                nc.scalar.preload_act_table_set("natural_log_exp_and_others")
            retire(U_OUT + 7)

        def dve_block(dve, b, last):
            def retire(u):
                p1_retire_lo(dve, b, u)

            nc.vector.tensor_copy(keys[:, 0, 0:CH], keys[:, BT, 0:CH])
            nc.vector.tensor_copy(v_prev[0:CH, 0, :], v_prev[0:CH, BT, :]).then_inc(carried, 1)
            for u in range(3):
                retire(u)
            dve.wait_ge(carried, b + 1)
            for t in range(BT):
                dve.wait_ge(dense_done, quarter(b, U_NARROW + 3, t))
                nc.vector.tensor_copy(v_prev[0:CH, t + 1, :], dense[CH:P, t, SV:SV + P])
                nc.vector.tensor_copy(narrow[:, t, :], dense[:, t, 0:NARROW]).then_inc(narrow_out, 1)
            retire(3)
            retire(4)
            retire(5)
            dve.wait_ge(gate_act, 3 * b + 3)
            nc.vector.scalar_tensor_tensor(out=gate_b[:].rearrange("p (a n) -> p a n", a=2), in0=aux[:, 2:4, :],
                                           scalar=0.0, in1=gate_a[:].rearrange("p (a n) -> p a n", a=2),
                                           op0=ALU.min, op1=ALU.subtract).then_inc(la_ready, 1)
            retire(6)
            retire(7)
            dve.wait_ge(decay_exp, 2 * b + 2)
            nc.vector.tensor_tensor(gate_b[:].rearrange("p (t n) -> p t n", t=BT), narrow[:, :, GK:GK + GH * DK],
                                    gate_a[:].rearrange("p (t n) -> p t n", t=BT), ALU.mult).then_inc(kdec_ready, 1)
            dve.wait_ge(dense_done, quarter(b, U_K, 3))
            kd = dense[:, 0, :].rearrange("p (t n) -> p t n", t=BT)
            nc.vector.tensor_copy(keys[:, 0:BT, PREV:KEYS], kd)
            nc.vector.tensor_copy(keys[:, 1:BT + 1, 0:CH], kd[:, :, CH:P]).then_inc(k_out, 1)
            retire(8)

            def row_max(s):
                r, hs = s % 2, s % 2
                dve.wait_ge(scores_ready, 8 * b + s + 1)
                nc.vector.tensor_reduce(smax[:, r, :].rearrange("p (g j) -> p g j", g=2),
                                        aux[:, 0:2, 0:2 * KEYS].rearrange("p g (j k) -> p g j k", j=2),
                                        AX_X, ALU.max).then_inc(smax_ready, 1)
                dve.wait_ge(smax_ready, 8 * b + s + 1)
                sk = nsink[:, hs * 4:hs * 4 + 4]
                nc.vector.scalar_tensor_tensor(out=nmax[:, r, :], in0=smax[:, r, :], scalar=-(DH ** -0.5), in1=sk,
                                               op0=ALU.mult, op1=ALU.min).then_inc(nmax_ready, 1)
                dve.wait_ge(nmax_ready, 16 * b + 2 * s + 1)
                nc.vector.tensor_tensor(esink_in[:, r, :], nmax[:, r, :], sk, ALU.subtract).then_inc(nmax_ready, 1)

            row_max(0)
            for s in range(8):
                t, hs, r = s // 2, s % 2, s % 2
                dve.wait_ge(pt_ready, 8 * b + s + 1)
                nc.vector.tensor_copy(pt_prev[:].rearrange("p i q -> p (i q)"), aux[0:PREV, 3, :]).then_inc(pt_prev_out, 1)
                if s < 7:
                    row_max(s + 1)
                dve.wait_ge(exp_done, 8 * b + s + 1)
                nc.vector.tensor_tensor(denom[:, r, :], rowsum[:, r, :], esink[:, r, :], ALU.add).then_inc(denom_ready, 1)
                dve.wait_ge(denom_ready, 16 * b + 2 * s + 1)
                nc.vector.reciprocal(rden[:, r, :], denom[:, r, :]).then_inc(denom_ready, 1)
                dve.wait_ge(denom_ready, 16 * b + 2 * s + 2)
                dve.wait_ge(pv_ready, 8 * b + s + 1)
                o = mix_swa[:, t, :].rearrange("p (g s j d) -> p g s j d", g=2, s=2, j=2)[:, :, hs, :, :]
                nc.vector.tensor_tensor(o.rearrange("p g j d -> p g j d"),
                                        aux[:, 2, 0:4 * DH].rearrange("p (g j d) -> p g j d", g=2, j=2),
                                        rden[:, r, :].rearrange("p (g j) -> p g j", g=2).unsqueeze(3)
                                        .to_broadcast([P, 2, 2, DH]), ALU.mult).then_inc(swa_out, 1)
                for c in range(3 + 3 * s, 6 + 3 * s):
                    if c < 24 and c % 4 == 3:
                        retire(U_GQ + c // 4)
            nc.vector.tensor_copy(mask[:, 0, :], mask[:, 1, :])
            retire(U_GG)

            for c in range(2 * BT):
                t, i = divmod(c, 2)
                if c % 4 == 0:
                    dve.wait_ge(u_ready, 2 * b + c // 4 + 1)
                    dve.wait_ge(decay_exp, 2 * b + 2)
                for p in range(2):
                    if p == 0 and c > 0:
                        dve.wait_ge(state_ready, 16 * b + 2 * c)
                    o = (t % 2) * 256 + p * DV
                    nc.vector.scalar_tensor_tensor(
                        out=state[:, c, p, :], in0=state[:, (c - 1) % (2 * BT), p, :],
                        scalar=chunk_g[:, t * 4 + p * 2 + i:t * 4 + p * 2 + i + 1],
                        in1=aux[:, 2 * i + t // 2, o:o + DV], op0=ALU.mult, op1=ALU.add).then_inc(state_ready, 1)
            retire(U_GG + 1)

            def o_evacuate(hf):
                dve.wait_ge(o_ready, 2 * b + hf + 1)
                nc.vector.tensor_copy(
                    gv_sb[:, 2 * hf:2 * hf + 2, :].rearrange("p t (a j v) -> p t a j v", a=2, j=2)[:, :, :, 1, :],
                    aux[:, 2 + hf, :].rearrange("p (t a v) -> p t a v", t=2, a=2)).then_inc(o_out_dve, 1)

            def o_squares(hf):
                dve.wait_ge(sq_ready, 2 * b + hf + 1)
                nc.vector.tensor_reduce(gss[:, 8 * hf:8 * hf + 8],
                                        q_sb[:, 2 * hf:2 * hf + 2, :].rearrange("p t (h v) -> p (t h) v", h=GH),
                                        AX_X, ALU.add).then_inc(gss_ready, 1)
                dve.wait_ge(gss_ready, 2 * b + hf + 1)
                c = slice(8 * hf, 8 * hf + 8)
                nc.vector.tensor_scalar(gms[:, c], gss[:, c], 1.0 / DV, EPS, ALU.mult, ALU.add).then_inc(gms_ready, 1)

            o_evacuate(0)
            retire(U_GG + 2)
            o_evacuate(1)
            o_squares(0)
            o_squares(1)

            def mix_evacuate(k):
                dve.wait_ge(mt_hi, KT_N * b + k + 1)
                nc.vector.tensor_tensor(mix_lo[:, k, :], aux[:, k % 4, :], mix_hi[:, k, :].bitcast(F32),
                                        ALU.subtract).then_inc(mt_lo, 1)

            for k in range(4):
                mix_evacuate(k)
            retire(U_GG + 3)
            for hf in range(2):
                dve.wait_ge(grs_ready, 2 * b + hf + 1)
                dve.wait_ge(o_out_act, 2 * b + hf + 1)
                v = gv_sb[:, 2 * hf:2 * hf + 2, :].rearrange("p t (h v) -> p (t h) v", h=GH)
                nc.vector.tensor_tensor(v, v, grs[:, 8 * hf:8 * hf + 8].unsqueeze(2).to_broadcast([P, 8, DV]),
                                        ALU.mult).then_inc(gla_scaled, 1)
            for hf in range(2):
                dve.wait_ge(gla_scaled, 2 * b + hf + 1)
                dve.wait_ge(sgw_ready, BT * b + 2 * hf + 2)
                nc.vector.tensor_tensor(gv_sb[:, 2 * hf:2 * hf + 2, :], gv_sb[:, 2 * hf:2 * hf + 2, :],
                                        sg[:, 2 * hf:2 * hf + 2, :], ALU.mult).then_inc(gla_out, 1)
            retire(U_OUT)
            retire(U_OUT + 1)
            for k in range(4, 8):
                mix_evacuate(k)
            if not last:
                norm1_mean(dve, b + 1)
                norm1_scale(dve, b + 1)
            retire(U_OUT + 2)

            def residual(half):
                dve.wait_ge(xr_in, 16 * (2 * b + half + 1))
                for t in range(BT):
                    dve.wait_ge(dense_done, quarter(b, U_OUT + 4 * half + 3, t))
                    nc.vector.tensor_tensor(xr[:, t, :], dense[:, t, :], xr[:, t, :], ALU.add).then_inc(res_added, 1)

            residual(0)
            retire(U_OUT + 3)
            retire(U_OUT + 4)
            if not last:
                for k in range(4):
                    norm1_lo(dve, b + 1, k)
            retire(U_OUT + 5)
            retire(U_OUT + 6)
            if not last:
                for k in range(4, 8):
                    norm1_lo(dve, b + 1, k)
            residual(1)
            retire(U_OUT + 7)

        def pool_block(pool, b, last):
            for hf in range(2):
                c = slice(8 * hf, 8 * hf + 8)
                pool.wait_ge(gms_ready, 2 * b + hf + 1)
                nc.gpsimd.tensor_tensor(grs[:, c], gms[:, c], neg_half[:, c], ALU.pow).then_inc(grs_ready, 1)
            for t in range(BT):
                pool.wait_ge(gg_out, BT * b + t + 1)
                v = sg[:, t, :].rearrange("p (h v) -> p h v", h=GH)
                nc.gpsimd.tensor_tensor(v, v, gwb[:].unsqueeze(1).to_broadcast([P, GH, DV]),
                                        ALU.mult).then_inc(sgw_ready, 1)
            if not last:
                norm1_rstd(pool, b + 1)

        def run_blocks(eng, program):
            with eng.Fori(0, BLOCKS - 1) as b:
                program(eng, b, False)
            program(eng, BLOCKS - 1, True)

        with nc.Block() as block:
            @block.sync
            def _(sp):
                load_xr(sp, 0, 0)
                for u in range(RING):
                    p1_retire_load(sp, 0, u, False)
                run_blocks(sp, sp_block)

            @block.tensor
            def _(pe):
                run_blocks(pe, pe_block)

            @block.scalar
            def _(act):
                nc.scalar.preload_act_table_set("natural_log_exp_and_others")
                run_blocks(act, act_block)

            @block.vector
            def _(dve):
                nc.vector.memset(rank_t[:], 1.0)
                run_blocks(dve, dve_block)

            @block.gpsimd
            def _(pool):
                run_blocks(pool, pool_block)
        mixer.close()

        ffn = outer.enter_context(ExitStack())
        ST = 2 * BT
        h = [alloc(ffn, f"h{i}", [P, 2, 2, BT, HALF]) for i in range(SUPER)]
        hs = alloc(ffn, "hs", [P, BT, HALF])
        n2_hi = alloc(ffn, "n2_hi", [P, KT_N, 2 * BLK], F32R)
        n2_lo = alloc(ffn, "n2_lo", [P, KT_N, 2 * BLK], F32R)
        a_hi = [alloc(ffn, f"a_hi{i}", [P, 2 * BLK], F32R) for i in range(2)]
        a_lo = [alloc(ffn, f"a_lo{i}", [P, 2 * BLK], F32R) for i in range(2)]
        gate_s = alloc(ffn, "gate_s", [P, 2, BLK])
        a_f = alloc(ffn, "a_f", [P, 2, BLK])
        fwb = alloc(ffn, "fwb", [P, D])
        ss2 = alloc(ffn, "ss2", [P, 2 * SUPER, ST])
        ms2 = alloc(ffn, "ms2", [P, 2 * SUPER, ST])
        rs2 = alloc(ffn, "rs2", [P, 2 * SUPER, ST])

        h_in = [sem(f"h_in{i}") for i in range(SUPER)]
        fw_in = sem("fw_in")
        ss2_ready = sem("ss2_ready")
        ms2_ready = sem("ms2_ready")
        rs2_ready = sem("rs2_ready")
        hs_ready = sem("hs_ready")
        ht_ready = sem("ht_ready")
        n2_hi_ready = sem("n2_hi_ready")
        n2_lo_ready = sem("n2_lo_ready")
        silu_done = sem("silu_done")
        mul_done = sem("mul_done")
        act_hi = sem("act_hi")
        act_lo = sem("act_lo")
        h_added = sem("h_added")
        fin_ready = sem("fin_ready")
        stored = sem("stored")
        GP = 8 + 2 * ST
        NORMS = (0, 1, 2, 3)

        def norm2_squares(act, turn, sb):
            which = turn
            for bb in range(2):
                for t in range(BT):
                    if turn + bb + t > 0:
                        act.wait_ge(ss2_ready, ST * turn + bb * BT + t)
                    ins = nc.scalar.activation(junk[:].rearrange("p (a n) -> p a n", a=2), h[sb][:, bb, :, t, :],
                                               ACT.Square, accum_out=ss2[:, which, bb * BT + t:bb * BT + t + 1])
                    ins.then_inc(ss2_ready, 1)

        def norm2_rstd(pool, which, turn):
            pool.wait_ge(ss2_ready, ST * turn)
            nc.gpsimd.tensor_scalar(ms2[:, which, :], ss2[:, which, :], 1.0 / D, EPS,
                                    ALU.mult, ALU.add).then_inc(ms2_ready, 1)
            pool.wait_ge(ms2_ready, turn)
            nc.gpsimd.tensor_tensor(rs2[:, which, :], ms2[:, which, :], neg_half[:, 0:ST],
                                    ALU.pow).then_inc(rs2_ready, 1)

        def group_pe(pe, sb, g):
            G = GROUPS * sb + g
            n = UNITS * BLOCKS + 6 * G
            for fi in range(2):
                for up in range(2):
                    u = 2 * fi + up
                    pe.wait_ge(w_lo_ready, n + u + 1)
                    if fi == 1:
                        pe.wait_ge(mul_done if up else silu_done, 2 * (2 * G + fi))
                    for th in range(2):
                        for k in range(KT_N):
                            w = slice(k * P, (k + 1) * P)
                            m = slice(th * BLK, (th + 1) * BLK)
                            ins = three_pass(aux[:, 2 * up + th, :], w_hi[u % RING][:, w], w_lo[u % RING][:, w],
                                             n2_hi[:, k, m], n2_lo[:, k, m], k == 0, k == KT_N - 1)
                        ins.then_inc(ffn_done, 1)
            pe.wait_ge(w_lo_ready, n + 6)
            for o in range(2 * ST):
                tile, nn = divmod(o, 2)
                if o % ST == 0:
                    pe.wait_ge(act_lo, 2 * (2 * G + 1) + o // ST + 1)
                if o > 3:
                    pe.wait_ge(h_added, 2 * ST * G + o - 3)
                for fi in range(2):
                    s = (4 + fi) % RING
                    ins = three_pass(dense[:, o % 4, :], a_hi[fi][:, tile * P:(tile + 1) * P],
                                     a_lo[fi][:, tile * P:(tile + 1) * P], w_hi[s][:, nn * HALF:(nn + 1) * HALF],
                                     w_lo[s][:, nn * HALF:(nn + 1) * HALF], fi == 0, fi == 1)
                ins.then_inc(ffn_done, 1)

        def unit_pieces(u):
            return 2 * u + 2 if u < 4 else GP

        def group_act(act, sb, g, final):
            G = GROUPS * sb + g

            def retire(u):
                if not (final and u >= 3):
                    act.wait_ge(ffn_done, GP * G + unit_pieces(u))
                    split_hi(act, 0, u % RING, (UNITS * BLOCKS) // RING + 2 * G + u // RING + 1)

            for fi in range(2):
                F = 2 * G + fi
                for th in range(2):
                    act.wait_ge(ffn_done, GP * G + 4 * fi + th + 1)
                    nc.scalar.activation(gate_s[:, th, :], aux[:, th, :], ACT.Silu).then_inc(silu_done, 1)
                retire(2 * fi)
                for th in range(2):
                    act.wait_ge(mul_done, 2 * F + th + 1)
                    nc.scalar.activation(a_hi[fi][:, th * BLK:(th + 1) * BLK], a_f[:, th, :],
                                         ACT.Copy).then_inc(act_hi, 1)
                retire(2 * fi + 1)
            retire(4)
            retire(5)

        def group_dve(dve, sb, g, final):
            G = GROUPS * sb + g
            n = UNITS * BLOCKS + 6 * G

            def retire(u):
                if not (final and u >= 3):
                    split_lo(dve, n + u + RING, u % RING)

            for fi in range(2):
                F = 2 * G + fi
                retire(2 * fi)
                for th in range(2):
                    m = slice(th * BLK, (th + 1) * BLK)
                    dve.wait_ge(ffn_done, GP * G + 4 * fi + 2 + th + 1)
                    dve.wait_ge(silu_done, 2 * F + th + 1)
                    nc.vector.tensor_tensor(a_f[:, th, :], aux[:, 2 + th, :], gate_s[:, th, :],
                                            ALU.mult).then_inc(mul_done, 1)
                    dve.wait_ge(act_hi, 2 * F + th + 1)
                    nc.vector.tensor_tensor(a_lo[fi][:, m], a_f[:, th, :], a_hi[fi][:, m].bitcast(F32),
                                            ALU.subtract).then_inc(act_lo, 1)
                retire(2 * fi + 1)
            for o in range(2 * ST):
                tile, nn = divmod(o, 2)
                bb, t = divmod(tile, BT)
                dve.wait_ge(ffn_done, GP * G + 8 + o + 1)
                dst = h[sb][:, bb, nn, t, :]
                nc.vector.tensor_tensor(dst, dense[:, o % 4, :], dst, ALU.add).then_inc(h_added, 1)
            retire(4)
            retire(5)

        def group_sp(sp, sb, g, final):
            G = GROUPS * sb + g
            for u in range(6):
                if final and u >= 3:
                    break
                sp.wait_ge(w_lo_ready, UNITS * BLOCKS + 6 * G + u + 1)
                wraps = u >= 3 and isinstance(g, int) and g == GROUPS - 1
                load_unit(sp, u % RING, w_ffn[u - 3] if wraps else w_ffn[6 * g + u + RING])

        def run_groups(eng, sb, program, *more):
            with eng.Fori(0, GROUPS - 1) as g:
                program(eng, sb, g, *more)
            program(eng, sb, GROUPS - 1, *[sb == SUPER - 1 for _ in more])

        def final_dve(dve, sb):
            dve.wait_ge(rs2_ready, SUPER + sb + 1)
            if sb == 0:
                dve.wait_ge(fw_in, 16)
            for bb in range(2):
                for t in range(BT):
                    v = h[sb][:, bb, :, t, :]
                    c = bb * BT + t
                    nc.vector.scalar_tensor_tensor(out=v, in0=v, scalar=rs2[:, SUPER + sb, c:c + 1],
                                                   in1=fwb[:].rearrange("p (a n) -> p a n", a=2),
                                                   op0=ALU.mult, op1=ALU.mult).then_inc(fin_ready, 1)

        def final_store(eng, sb):
            for bb in range(2):
                for t in range(BT):
                    eng.wait_ge(fin_ready, ST * sb + bb * BT + t + 1)
                    eng.dma_start(out[2 * sb + bb][:, t, :].rearrange("p (a n) -> p a n", a=2),
                                  h[sb][:, bb, :, t, :]).then_inc(stored, 16)

        with nc.Block() as block:
            @block.sync
            def _(sp):
                for sb in range(SUPER):
                    for bb in range(2):
                        for nn in range(2):
                            sp.dma_start(h[sb][:, bb, nn, :, :].rearrange("p t n -> p (t n)"),
                                         h_mid[4 * sb + 2 * bb + nn]).then_inc(h_in[sb], 16)
                sp.dma_start(fwb[:], fw).then_inc(fw_in, 16)
                for sb in range(SUPER):
                    run_groups(sp, sb, group_sp, False)

            @block.tensor
            def _(pe):
                for sb in range(SUPER):
                    for r in range(4):
                        bb, nn = divmod(r, 2)
                        pe.wait_ge(hs_ready, 4 * sb + r + 1)
                        for kk in range(4):
                            if r > 0:
                                pe.wait_ge(n2_lo_ready, 16 * sb + 4 * (r - 1) + kk + 1)
                            elif sb > 0 and kk == 0:
                                pe.wait_ge(h_added, 2 * ST * GROUPS * sb)
                            for t in range(BT):
                                ins = nc.tensor.transpose(dense[:, kk, t * P:(t + 1) * P],
                                                          hs[:, t, kk * P:(kk + 1) * P], ident)
                            ins.then_inc(ht_ready, 1)
                    pe.wait_ge(n2_lo_ready, 16 * (sb + 1))
                    run_groups(pe, sb, group_pe)

            @block.scalar
            def _(act):
                nc.scalar.preload_act_table_set("silu_and_others")
                for sb in range(SUPER):
                    act.wait_ge(h_in[sb], 64)
                    norm2_squares(act, sb, sb)
                for sb in range(SUPER):
                    for r in range(4):
                        bb, nn = divmod(r, 2)
                        for kk in range(4):
                            k = 4 * nn + kk
                            act.wait_ge(ht_ready, 16 * sb + 4 * r + kk + 1)
                            nc.scalar.activation(n2_hi[:, k, bb * BLK:(bb + 1) * BLK], dense[:, kk, :], ACT.Copy,
                                                 scale=n2[:, k:k + 1]).then_inc(n2_hi_ready, 1)
                    run_groups(act, sb, group_act, False)
                    act.wait_ge(h_added, 2 * ST * GROUPS * (sb + 1))
                    norm2_squares(act, SUPER + sb, sb)

            @block.gpsimd
            def _(pool):
                for turn in range(2 * SUPER):
                    norm2_rstd(pool, turn, turn + 1)
                for sb in range(SUPER):
                    final_store(pool, sb)
                pool.wait_ge(stored, 16 * SUPER * ST)

            @block.vector
            def _(dve):
                for sb in range(SUPER):
                    for r in range(4):
                        bb, nn = divmod(r, 2)
                        dve.wait_ge(rs2_ready, sb + 1)
                        if sb + r > 0:
                            dve.wait_ge(ht_ready, 16 * sb + 4 * r)
                        for t in range(BT):
                            ins = nc.vector.tensor_scalar(hs[:, t, :], h[sb][:, bb, nn, t, :],
                                                          rs2[:, sb, bb * BT + t:bb * BT + t + 1], None, ALU.mult)
                        ins.then_inc(hs_ready, 1)
                        for kk in range(4):
                            k = 4 * nn + kk
                            m = slice(bb * BLK, (bb + 1) * BLK)
                            dve.wait_ge(n2_hi_ready, 16 * sb + 4 * r + kk + 1)
                            nc.vector.scalar_tensor_tensor(out=n2_lo[:, k, m], in0=dense[:, kk, :],
                                                           scalar=n2[:, k:k + 1], in1=n2_hi[:, k, m].bitcast(F32),
                                                           op0=ALU.mult, op1=ALU.subtract).then_inc(n2_lo_ready, 1)
                    run_groups(dve, sb, group_dve, False)
                    final_dve(dve, sb)
        ffn.close()


def pack(w, rows, cols):
    import numpy as np
    k = w.shape[0] // P
    return np.ascontiguousarray(w.reshape(k // rows, rows, P, cols).transpose(0, 2, 1, 3)).reshape(k // rows, P, -1)


def kernel(x, meta_tokens, norm1_w, w_in, gla_gate_w2, gla_gate_b, gla_norm_w, swa_sinks, w_out,
           norm2_w, w_gate, w_up, w_down, final_norm_w):
    import numpy as np
    import concourse.bacc as bacc
    from concourse.bass_utils import run_bass_kernel_spmd

    w_in, w_out = np.asarray(w_in)[0], np.asarray(w_out)[0]
    w_gate, w_up, w_down = np.asarray(w_gate)[0], np.asarray(w_up)[0], np.asarray(w_down)[0]
    narrow = np.zeros((D, HALF), w_in.dtype)
    narrow[:, SV:SV + P] = w_in[:, 640:768]
    narrow[:, GK:GK + 256] = w_in[:, 1024:1280]
    narrow[:, GLR:GLR + RANK] = w_in[:, 2304:2320]
    units = [pack(narrow, 2, HALF)]
    for j in range(4):
        pair = np.concatenate([w_in[:, j * DH:(j + 1) * DH], w_in[:, (4 + j) * DH:(5 + j) * DH]], axis=1)
        units.append(pack(pair, 8, P))
    units.append(pack(w_in[:, 512:640], 8, P))
    for j in range(2):
        units.append(pack(w_in[:, 768 + j * P:768 + (j + 1) * P], 8, P))
    units += [pack(w_in[:, 1280:1792], 2, HALF), pack(w_in[:, 1792:2304], 2, HALF)]
    units += [pack(w_out[:, 0:HALF], 2, HALF), pack(w_out[:, HALF:D], 2, HALF)]
    w_block = np.concatenate(units)
    units = []
    for g in range(GROUPS):
        for f in (2 * g, 2 * g + 1):
            for w in (w_gate, w_up):
                units.append(pack(w[:, f * P:(f + 1) * P], 8, P))
        units.append(w_down[2 * g * P:2 * (g + 1) * P].reshape(2, P, D))
    w_ffn = np.concatenate(units)

    consts = np.zeros((P, CONSTS), np.float32)
    masks = np.zeros((P, MASKS), np.float32)
    i = np.arange(P)
    consts[:, C_ID:C_ID + P] = np.eye(P)
    same = i[:, None] // CH == i[None, :] // CH
    consts[:, C_TRI:C_TRI + P] = np.where(same & (i[:, None] > i[None, :]), 1 / 16, 0)
    for c in range(2):
        consts[c * CH:(c + 1) * CH, C_CHUNK + c] = 1 / 16
        for r in (0, DH):
            masks[r + c, M_ROW + c * CH:M_ROW + (c + 1) * CH] = 1
    for r in (0, DH):
        for c in (M_MASK, M_MASK0):
            masks[r, c + KEYS - CH:c + KEYS] = -1e30
            masks[r + 1, c:c + CH] = -1e30
        masks[r, M_MASK0:M_MASK0 + CH] = -1e30

    def tiles(w):
        return np.ascontiguousarray(np.asarray(w).reshape(KT_N, P).T)

    def rows(w):
        w = np.asarray(w).reshape(1, -1)
        return np.ascontiguousarray(np.broadcast_to(w, (P, w.shape[1])))

    arrays = {
        "x": np.ascontiguousarray(np.asarray(x)).reshape(BLOCKS, BT, P, D),
        "meta": np.ascontiguousarray(meta_tokens),
        "n1w": tiles(norm1_w), "n2w": tiles(norm2_w), "fw": rows(final_norm_w),
        "w_block": w_block, "w_ffn": w_ffn,
        "w2b": np.concatenate([np.asarray(gla_gate_w2)[0], np.asarray(gla_gate_b).reshape(1, -1)]),
        "gw": rows(gla_norm_w), "sinks": rows(swa_sinks), "consts": consts, "masks": masks,
    }
    nc = bacc.Bacc("TRN2", target_bir_lowering=False, num_devices=1)
    args = {n: nc.dram_tensor(f"in_{n}", a.shape, F32, kind="ExternalInput").ap() for n, a in arrays.items()}
    h_mid = nc.dram_tensor("h_mid", (2 * BLOCKS, P, BT * HALF), F32).ap()
    out = nc.dram_tensor("out_0", (BLOCKS, BT, P, D), F32, kind="ExternalOutput").ap()
    args["x"] = args["x"].rearrange("b t p d -> b p t d")
    build(nc, h_mid=h_mid, out=out.rearrange("b t p d -> b p t d"), **args)
    r = run_bass_kernel_spmd(nc, [{f"in_{n}": a for n, a in arrays.items()}], core_ids=[0])
    return r.results[0]["out_0"].reshape(1, BLOCKS * BLK, D)
```

```python
from contextlib import ExitStack

import concourse.bass as bass
from concourse import mybir

F32 = mybir.dt.float32
F32R = mybir.dt.float32r
BF16 = mybir.dt.bfloat16
ALU = mybir.AluOpType
ACT = mybir.ActivationFunctionType
AX_X = mybir.AxisListType.X

P = 128
D = 1024
KT_N = D // P
CH = 64
META = 16
DH = 64
WIN = CH + META + CH
PREV = CH + META
QH = 8
GH = 4
DK = 64
DV = 128
BT = 4
BLK = BT * P
BLOCKS = 4
SUPER = 2
F_TILES = 22
GROUPS = F_TILES // 2
HALF = 512
UNIT = 1024
RING = 3
RANK = 16
EPS = 1e-6
SV, GK, GLR = 0, 128, 384
NARROW = 400
N_GK, N_GLR = GK - P, GLR - P
U_NARROW, U_Q, U_K, U_GQ, U_GV, U_GG, U_OUT = 0, 4, 8, 9, 11, 15, 19
UNITS = 27
FFN_UNITS = 6 * GROUPS
C_ID, C_TRI, C_CHUNK, CONSTS = 0, 128, 256, 258
M_ROW, M_MASK, MASKS = 0, CH, CH + WIN


def quarter(b, u, c):
    return 4 * (UNITS * b + u) + c + 1


def build(nc, x, meta, n1w, n2w, fw, w_block, w_ffn, w2b, gw, sinks, consts, masks, h_mid, out):
    with ExitStack() as outer:
        def alloc(stack, name, shape, dt=F32):
            return stack.enter_context(nc.sbuf_tensor(name, shape, dt))

        def sem(name):
            return outer.enter_context(nc.semaphore(name))

        stage = [alloc(outer, f"stage{i}", [P, UNIT]) for i in range(RING)]
        w_hi = [alloc(outer, f"w_hi{i}", [P, UNIT], F32R) for i in range(RING)]
        w_lo = [alloc(outer, f"w_lo{i}", [P, UNIT], F32R) for i in range(RING)]
        cst = alloc(outer, "cst", [P, CONSTS])
        n1 = alloc(outer, "n1", [P, KT_N])
        n2 = alloc(outer, "n2", [P, KT_N])
        junk = alloc(outer, "junk", [P, D], BF16)
        xn = alloc(outer, "xn", [P, BT, D])
        hn_hi = alloc(outer, "hn_hi", [P, KT_N, BLK], F32R)
        hn_lo = alloc(outer, "hn_lo", [P, KT_N, BLK], F32R)
        ssh = alloc(outer, "ssh", [P, 2, BLOCKS, BT])
        ms2 = alloc(outer, "ms2", [P, 2, BLOCKS, BT])
        rs2 = alloc(outer, "rs2", [P, 2, BLOCKS, BT])
        neg_half = alloc(outer, "neg_half", [P, GH * BT])
        dense = outer.enter_context(nc.psum_tensor("dense", [P, 4, HALF], F32))
        aux = outer.enter_context(nc.psum_tensor("aux", [P, 4, HALF], F32))
        ident = cst[:, C_ID:C_ID + P]
        tri = cst[:, C_TRI:C_TRI + P]

        c_in = sem("c_in")

        def wait_alone(eng, *waits):
            for _, value in waits:
                eng.compute_val(value)
            eng.wait_ge(c_in, 16 * 7)
            for signal, value in waits:
                eng.wait_ge(signal, value)

        w_loaded = [sem(f"w_loaded{i}") for i in range(RING)]
        w_hi_ready = sem("w_hi_ready")
        w_lo_ready = sem("w_lo_ready")
        dense_done = sem("dense_done")
        ffn_done = sem("ffn_done")

        def load_unit(sp, slot, src):
            sp.dma_start(stage[slot][:], src).then_inc(w_loaded[slot], 16)

        def split_hi(act, n, slot, round_):
            act.wait_ge(w_loaded[slot], 16 * (round_ + 1))
            nc.scalar.activation(w_hi[slot][:], stage[slot][:], ACT.Copy).then_inc(w_hi_ready, 1)

        def split_lo(dve, n, slot):
            dve.wait_ge(w_hi_ready, n + 1)
            nc.vector.tensor_tensor(w_lo[slot][:], stage[slot][:], w_hi[slot][:].bitcast(F32),
                                    ALU.subtract).then_inc(w_lo_ready, 1)

        def three_pass(out_ap, a_hi, a_lo, b_hi, b_lo, first, last):
            nc.tensor.matmul(out_ap, a_hi, b_lo, start=first, stop=False)
            nc.tensor.matmul(out_ap, a_lo, b_hi, start=False, stop=False)
            return nc.tensor.matmul(out_ap, a_hi, b_hi, start=False, stop=last)

        x0_in = [sem(f"x0_in{t}") for t in range(BT)]
        x_in = sem("x_in")
        ss1_ready = sem("ss1_ready")
        ms1_ready = sem("ms1_ready")
        rstd1_ready = sem("rstd1_ready")
        xn_ready = sem("xn_ready")
        xt_ready = sem("xt_ready")
        xt_hi = sem("xt_hi")
        xt_lo = sem("xt_lo")
        xr_in = sem("xr_in")
        h_stored = sem("h_stored")
        h_sq = sem("h_sq")
        h_in = [sem(f"h_in{b}") for b in range(BLOCKS)]
        h_sum = sem("h_sum")
        ms2_ready = sem("ms2_ready")
        rs2_ready = sem("rs2_ready")

        def norm2_rstd(pool, turn, blocks):
            c = slice(blocks[0], blocks[-1] + 1)
            nc.gpsimd.tensor_tensor(ms2[:, 0, c, :], ssh[:, 0, c, :], ssh[:, 1, c, :], ALU.add).then_inc(h_sum, 1)
            pool.wait_ge(h_sum, turn + 1)
            nc.gpsimd.tensor_scalar(ms2[:, 0, c, :], ms2[:, 0, c, :], 1.0 / D, EPS,
                                    ALU.mult, ALU.add).then_inc(ms2_ready, 1)
            pool.wait_ge(ms2_ready, turn + 1)
            nc.gpsimd.tensor_tensor(rs2[:, 0, c, :], ms2[:, 0, c, :],
                                    neg_half[:, 0:BT * len(blocks)].rearrange("p (b t) -> p b t", t=BT),
                                    ALU.pow).then_inc(rs2_ready, 1)

        mixer = outer.enter_context(ExitStack())
        ss1 = alloc(mixer, "ss1", [P, BT])
        ms1 = alloc(mixer, "ms1", [P, BT])
        rstd1 = alloc(mixer, "rstd1", [P, BT])
        keys = alloc(mixer, "keys", [P, 2 * BT + 1, PREV])
        values = alloc(mixer, "values", [PREV, 2 * BT + 1, P])
        state = alloc(mixer, "state", [P, 2 * BT, 2, DV])
        w2 = alloc(mixer, "w2", [RANK + 1, GH * DK])
        row_ind = alloc(mixer, "row_ind", [P, CH], BF16)
        mask = alloc(mixer, "mask", [P, WIN], BF16)
        nsink = alloc(mixer, "nsink", [P, QH])
        sinkb = alloc(mixer, "sinkb", [P, QH])
        sinki = alloc(mixer, "sinki", [P, QH])
        gwb = alloc(mixer, "gwb", [P, DV])

        def load_x(eng, b):
            eng.dma_start(xn[:], x[b]).then_inc(x_in, 16)

        def norm1_squares(act, b):
            for t in range(BT):
                if isinstance(b, int) and b == 0:
                    act.wait_ge(x0_in[t], 16)
                elif t == 0:
                    act.wait_ge(x_in, 16 * b)
                if t > 0:
                    act.wait_ge(ss1_ready, BT * b + t)
                nc.scalar.activation(junk[:], xn[:, t, :], ACT.Square,
                                     accum_out=ss1[:, t:t + 1]).then_inc(ss1_ready, 1)

        def norm1_rstd(pool, b):
            pool.wait_ge(ms1_ready, BT + b)
            nc.gpsimd.tensor_tensor(rstd1[:], ms1[:], neg_half[:, 0:BT], ALU.pow).then_inc(rstd1_ready, 1)

        def norm1_mean(dve, b):
            dve.wait_ge(ss1_ready, BT * b + BT)
            nc.vector.tensor_scalar(ms1[:], ss1[:], 1.0 / D, EPS, ALU.mult, ALU.add).then_inc(ms1_ready, 1)

        def norm1_scale(dve, b):
            dve.wait_ge(rstd1_ready, BT + b)
            for t in range(BT):
                nc.vector.tensor_scalar(xn[:, t, :], xn[:, t, :], rstd1[:, t:t + 1], None,
                                        ALU.mult).then_inc(xn_ready, 1)

        def norm1_mean0(dve, t):
            dve.wait_ge(ss1_ready, t + 1)
            nc.vector.tensor_scalar(ms1[:, t:t + 1], ss1[:, t:t + 1], 1.0 / D, EPS,
                                    ALU.mult, ALU.add).then_inc(ms1_ready, 1)

        def norm1_rstd0(pool, t):
            pool.wait_ge(ms1_ready, t + 1)
            nc.gpsimd.tensor_tensor(rstd1[:, t:t + 1], ms1[:, t:t + 1], neg_half[:, 0:1],
                                    ALU.pow).then_inc(rstd1_ready, 1)

        def norm1_scale0(dve, t):
            dve.wait_ge(rstd1_ready, t + 1)
            nc.vector.tensor_scalar(xn[:, t, :], xn[:, t, :], rstd1[:, t:t + 1], None,
                                    ALU.mult).then_inc(xn_ready, 1)

        def norm1_transpose(pe, b, k):
            for t in range(BT):
                last = nc.tensor.transpose(aux[:, k % 4, t * P:(t + 1) * P], xn[:, t, k * P:(k + 1) * P], ident)
            last.then_inc(xt_ready, 1)

        def norm1_hi(act, b, k, weight):
            act.wait_ge(xt_ready, KT_N * b + k + 1)
            nc.scalar.activation(hn_hi[:, k, :], aux[:, k % 4, :], ACT.Copy,
                                 scale=weight[:, k:k + 1]).then_inc(xt_hi, 1)

        def norm1_lo(dve, b, k, weight):
            dve.wait_ge(xt_hi, KT_N * b + k + 1)
            nc.vector.scalar_tensor_tensor(out=hn_lo[:, k, :], in0=aux[:, k % 4, :], scalar=weight[:, k:k + 1],
                                           in1=hn_hi[:, k, :].bitcast(F32), op0=ALU.mult,
                                           op1=ALU.subtract).then_inc(xt_lo, 1)

        with ExitStack() as st:
            WK, WN3, WV, WMETA = 0, 1, 2, 6
            wm = alloc(st, "wm", [P, WMETA, UNIT])
            mx = alloc(st, "mx", [META, D])
            masks_in = alloc(st, "masks_in", [P, MASKS])
            mss = alloc(st, "mss", [META, 1])
            mms = alloc(st, "mms", [META, 1])
            mrs = alloc(st, "mrs", [META, 1])
            mt = alloc(st, "mt", [P, KT_N, META])
            mn = alloc(st, "mn", [META, NARROW])
            mv = alloc(st, "mv", [META, GH * DV])
            mg = alloc(st, "mg", [RANK + 1, META])
            ga = alloc(st, "ga", [META, GH * DK])
            gb = alloc(st, "gb", [META, GH * DK])
            m_in = sem("m_in")
            mw_in = sem("mw_in")
            mwv_in = sem("mwv_in")
            m_square = sem("m_square")
            m_gate_act = sem("m_gate_act")
            m_pool = sem("m_pool")
            zeros = sem("zeros")
            m_scaled = sem("m_scaled")
            m_normed = sem("m_normed")
            sinks_ready = sem("sinks_ready")
            mn_out = sem("mn_out")
            mg_out = sem("mg_out")
            m_la = sem("m_la")
            m_kdec = sem("m_kdec")
            state0 = sem("state0")
            m_transposed = sem("m_transposed")
            m_narrow = sem("m_narrow")
            m_keys = sem("m_keys")
            m_rank = sem("m_rank")
            m_logit = sem("m_logit")
            m_values = sem("m_values")
            m_decay = sem("m_decay")
            m_update = sem("m_update")
            with nc.Block() as block:
                @block.sync
                def _(sp):
                    sp.dma_start(mx[:], meta).then_inc(m_in, 16)
                    for t in range(BT):
                        sp.dma_start(xn[:, t, :], x[0][:, t, :]).then_inc(x0_in[t], 16)
                    for dst, src in ((cst, consts), (masks_in, masks), (n1, n1w), (n2, n2w), (w2, w2b), (gwb, gw), (sinki, sinks)):
                        sp.dma_start(dst[:], src).then_inc(c_in, 16)
                    for u in range(RING):
                        load_unit(sp, u, w_block[u])
                    for i, u in enumerate((U_K, U_NARROW + 3, *range(U_GV, U_GV + 4))):
                        sp.dma_start(wm[:, i, :], w_block[u]).then_inc(mw_in if i < WV else mwv_in, 16)

                @block.scalar
                def _(act):
                    nc.scalar.preload_act_table_set("natural_log_exp_and_others")
                    act.wait_ge(m_in, 16)
                    nc.scalar.activation(junk[0:META, :], mx[:], ACT.Square, accum_out=mss[:]).then_inc(m_square, 1)
                    act.wait_ge(m_square, 1)
                    norm1_squares(act, 0)
                    act.wait_ge(c_in, 16 * 7)
                    for k in range(KT_N):
                        norm1_hi(act, 0, k, n1)
                    for u in range(RING):
                        split_hi(act, u, u, 0)
                    act.wait_ge(m_logit, 1)
                    nc.scalar.activation(ga[:], dense[0:META, 0, 0:GH * DK], ACT.Abs).then_inc(m_gate_act, 1)
                    act.wait_ge(m_gate_act, 1)
                    nc.scalar.activation(gb[:], ga[:], ACT.Exp, scale=-1.0).then_inc(m_gate_act, 1)
                    act.wait_ge(m_gate_act, 2)
                    nc.scalar.activation(ga[:], gb[:], ACT.Ln, bias=1.0).then_inc(m_gate_act, 1)
                    act.wait_ge(m_decay, 1)
                    nc.scalar.activation(ga[:], dense[0:META, 2, 0:GH * DK], ACT.Exp).then_inc(m_gate_act, 1)

                @block.gpsimd
                def _(pool):
                    nc.gpsimd.memset(neg_half[:], -0.5).then_inc(m_pool, 1)
                    pool.wait_ge(m_square, 1)
                    nc.gpsimd.tensor_scalar(mms[:], mss[:], 1.0 / D, EPS, ALU.mult, ALU.add).then_inc(m_pool, 1)
                    pool.wait_ge(m_pool, 2)
                    nc.gpsimd.tensor_tensor(mrs[:], mms[:], neg_half[0:META, 0:1], ALU.pow).then_inc(m_pool, 1)
                    for t in range(BT):
                        norm1_rstd0(pool, t)

                @block.vector
                def _(dve):
                    nc.vector.memset(mg[:], 1.0)
                    nc.vector.memset(keys[:, 2 * BT, 0:CH], 0.0)
                    nc.vector.memset(values[0:CH, 2 * BT, :], 0.0).then_inc(zeros, 1)
                    dve.wait_ge(m_pool, 3)
                    nc.vector.tensor_scalar(mx[:], mx[:], mrs[:], None, ALU.mult).then_inc(m_scaled, 1)
                    for t in range(BT):
                        norm1_mean0(dve, t)
                        norm1_scale0(dve, t)
                    dve.wait_ge(c_in, 16 * 7)
                    nc.vector.tensor_copy(row_ind[:], masks_in[:, M_ROW:M_ROW + CH])
                    nc.vector.tensor_copy(mask[:], masks_in[:, M_MASK:M_MASK + WIN])
                    nc.vector.tensor_copy(sinkb[:].rearrange("p (s g j) -> p s g j", s=2, g=2),
                                          sinki[:].rearrange("p (g s j) -> p s g j", s=2, g=2)).then_inc(sinks_ready, 1)
                    dve.wait_ge(sinks_ready, 1)
                    nc.vector.tensor_scalar(nsink[:], sinkb[:], -1.0, None, ALU.mult).then_inc(sinks_ready, 1)
                    dve.wait_ge(m_transposed, 1)
                    nc.vector.tensor_tensor(mt[:], dense[:, 0, 0:KT_N * META].rearrange("p (k m) -> p k m", k=KT_N),
                                            n1[:].unsqueeze(2).to_broadcast([P, KT_N, META]),
                                            ALU.mult).then_inc(m_normed, 1)
                    for k in range(KT_N):
                        norm1_lo(dve, 0, k, n1)
                    for u in range(RING):
                        split_lo(dve, u, u)
                    dve.wait_ge(m_narrow, 1)
                    nc.vector.tensor_copy(mn[:], dense[0:META, 2, 0:NARROW]).then_inc(mn_out, 1)
                    for c in range(2 * BT + 1):
                        nc.vector.tensor_copy(values[CH:PREV, c, :], dense[0:META, 2, SV:SV + P])
                    dve.wait_ge(m_rank, 1)
                    nc.vector.tensor_copy(mg[0:RANK, :], dense[0:RANK, 0, 0:META]).then_inc(mg_out, 1)
                    dve.wait_ge(m_keys, 1)
                    nc.vector.tensor_copy(keys[:, :, CH:PREV],
                                          dense[:, 1, 0:META].unsqueeze(1).to_broadcast([P, 2 * BT + 1, META]))
                    dve.wait_ge(m_gate_act, 3)
                    nc.vector.scalar_tensor_tensor(out=gb[:], in0=dense[0:META, 0, 0:GH * DK], scalar=0.0,
                                                   in1=ga[:], op0=ALU.min, op1=ALU.subtract).then_inc(m_la, 1)
                    dve.wait_ge(m_values, 1)
                    nc.vector.tensor_copy(mv[:], dense[0:META, 3, :])
                    dve.wait_ge(m_gate_act, 4)
                    nc.vector.tensor_tensor(gb[:], mn[:, GK:GK + GH * DK], ga[:], ALU.mult).then_inc(m_kdec, 1)
                    dve.wait_ge(m_update, 1)
                    nc.vector.tensor_copy(state[:, 2 * BT - 1, :, :],
                                          dense[:, 3, 0:2 * DV].rearrange("p (a v) -> p a v", a=2)).then_inc(state0, 1)

                @block.tensor
                def _(pe):
                    pe.wait_ge(c_in, 16 * 7)
                    pe.wait_ge(m_scaled, 1)
                    for k in range(KT_N):
                        last = nc.tensor.transpose(dense[:, 0, k * META:(k + 1) * META], mx[:, k * P:(k + 1) * P],
                                                   ident[0:META, 0:META])
                    last.then_inc(m_transposed, 1)
                    for t in range(BT):
                        pe.wait_ge(xn_ready, t + 1)
                        for k in range(4):
                            last = nc.tensor.transpose(aux[:, k, t * P:(t + 1) * P], xn[:, t, k * P:(k + 1) * P], ident)
                            if t == BT - 1:
                                last.then_inc(xt_ready, 1)
                    for k in range(4, KT_N):
                        pe.wait_ge(xt_lo, k - 3)
                        norm1_transpose(pe, 0, k)
                    pe.wait_ge(m_normed, 1)
                    for k in range(KT_N):
                        if k % 2 == 0 and k < 2 * RING:
                            pe.wait_ge(w_loaded[k // 2], 16)
                        if k == 2 * RING:
                            pe.wait_ge(mw_in, 16 * WV)
                        unit = stage[k // 2] if k < 2 * RING else wm[:, WN3, :]
                        last = nc.tensor.matmul(dense[0:META, 2, 0:NARROW], mt[:, k, :],
                                                unit[:, (k % 2) * HALF:(k % 2) * HALF + NARROW],
                                                start=k == 0, stop=k == KT_N - 1)
                    last.then_inc(m_narrow, 1)
                    for k in range(KT_N):
                        last = nc.tensor.matmul(dense[:, 1, 0:META], wm[:, WK, k * P:(k + 1) * P], mt[:, k, :],
                                                start=k == 0, stop=k == KT_N - 1)
                    last.then_inc(m_keys, 1)
                    pe.wait_ge(mn_out, 1)
                    nc.tensor.transpose(dense[0:RANK, 0, 0:META], mn[:, GLR:GLR + RANK],
                                        ident[0:META, 0:META]).then_inc(m_rank, 1)
                    pe.wait_ge(mwv_in, 16 * (WMETA - WV))
                    for k in range(KT_N):
                        if k == 4:
                            pe.wait_ge(mg_out, 1)
                            nc.tensor.matmul(dense[0:META, 0, 0:GH * DK], mg[:], w2[:],
                                             start=True, stop=True).then_inc(m_logit, 1)
                        last = nc.tensor.matmul(dense[0:META, 3, :], mt[:, k, :],
                                                wm[:, WV + k // 2, (k % 2) * HALF:(k % 2 + 1) * HALF],
                                                start=k == 0, stop=k == KT_N - 1)
                    last.then_inc(m_values, 1)
                    pe.wait_ge(m_la, 1)
                    nc.tensor.matmul(dense[0:META, 2, 0:GH * DK], tri[0:META, 0:META], gb[:],
                                     start=True, stop=True).then_inc(m_decay, 1)
                    pe.wait_ge(m_kdec, 1)
                    for h in range(GH):
                        last = nc.tensor.matmul(dense[(h % 2) * DK:(h % 2 + 1) * DK, 3, (h // 2) * DV:(h // 2 + 1) * DV],
                                                gb[:, h * DK:(h + 1) * DK], mv[:, h * DV:(h + 1) * DV],
                                                start=True, stop=True)
                    last.then_inc(m_update, 1)

        mx_st = mixer.enter_context(ExitStack())
        xr = alloc(mx_st, "xr", [P, BT, HALF])
        mix_hi = alloc(mx_st, "mix_hi", [P, KT_N, BLK], F32R)
        mix_lo = alloc(mx_st, "mix_lo", [P, KT_N, BLK], F32R)
        mix_swa = alloc(mx_st, "mix_swa", [P, BT, QH * DH])
        q_sb = alloc(mx_st, "q_sb", [P, 4, BLK])
        gq_sb = alloc(mx_st, "gq_sb", [P, 2, BLK])
        narrow = alloc(mx_st, "narrow", [P, BT, NARROW - P])
        gv_sb = alloc(mx_st, "gv_sb", [P, BT, GH * DV])
        sg = alloc(mx_st, "sg", [P, BT, GH * DV])
        gate_a = alloc(mx_st, "gate_a", [P, BT * GH * DK])
        gate_b = alloc(mx_st, "gate_b", [P, BT * GH * DK])
        rank_t = alloc(mx_st, "rank_t", [RANK + 1, BLK])
        chunk_g = alloc(mx_st, "chunk_g", [P, 4 * BT])
        gss = alloc(mx_st, "gss", [P, GH * BT])
        gms = alloc(mx_st, "gms", [P, GH * BT])
        grs = alloc(mx_st, "grs", [P, GH * BT])
        probs = alloc(mx_st, "probs", [P, 4, WIN])
        pt_own = alloc(mx_st, "pt_own", [CH, 4, P])
        pt_prev = alloc(mx_st, "pt_prev", [PREV, 4, P])
        smax = alloc(mx_st, "smax", [P, 2, 4])
        nmax = alloc(mx_st, "nmax", [P, 2, 4])
        esink_in = alloc(mx_st, "esink_in", [P, 2, 4])
        esink = alloc(mx_st, "esink", [P, 2, 4])
        rowsum = alloc(mx_st, "rowsum", [P, 2, 4])
        denom = alloc(mx_st, "denom", [P, 2, 4])
        rden = alloc(mx_st, "rden", [P, 2, 4])

        rank_ready = sem("rank_ready")
        logit_ready = sem("logit_ready")
        decay_ready = sem("decay_ready")
        scores_ready = sem("scores_ready")
        pt_ready = sem("pt_ready")
        pv_ready = sem("pv_ready")
        u_ready = sem("u_ready")
        o_ready = sem("o_ready")
        mt_ready = sem("mt_ready")
        q_out = sem("q_out")
        gq_out = sem("gq_out")
        gv_out = sem("gv_out")
        rank_out = sem("rank_out")
        gate_act = sem("gate_act")
        decay_exp = sem("decay_exp")
        exp_done = sem("exp_done")
        pt_own_out = sem("pt_own_out")
        o_out_act = sem("o_out_act")
        sq_ready = sem("sq_ready")
        gg_out = sem("gg_out")
        mt_hi = sem("mt_hi")
        carried = sem("carried")
        narrow_out = sem("narrow_out")
        k_out = sem("k_out")
        la_ready = sem("la_ready")
        kdec_ready = sem("kdec_ready")
        smax_ready = sem("smax_ready")
        nmax_ready = sem("nmax_ready")
        denom_ready = sem("denom_ready")
        pt_prev_out = sem("pt_prev_out")
        swa_out = sem("swa_out")
        state_ready = sem("state_ready")
        o_out_dve = sem("o_out_dve")
        gss_ready = sem("gss_ready")
        gms_ready = sem("gms_ready")
        gla_scaled = sem("gla_scaled")
        gla_out = sem("gla_out")
        mt_lo = sem("mt_lo")
        h0_added = sem("h0_added")
        h1_added = sem("h1_added")
        grs_ready = sem("grs_ready")
        sgw_ready = sem("sgw_ready")

        def next_unit(b, u, last):
            v = u + RING
            if v < UNITS:
                return w_block[v]
            return w_ffn[v - UNITS] if last else w_block[v - UNITS]

        def p1_retire_load(sp, b, u, last):
            sp.wait_ge(w_lo_ready, UNITS * b + u + 1)
            load_unit(sp, u % RING, next_unit(b, u, last))

        def p1_retire_hi(act, b, u):
            act.wait_ge(dense_done, quarter(b, u, 3))
            split_hi(act, UNITS * b + u + RING, u % RING, (UNITS // RING) * b + u // RING + 1)

        def p1_retire_lo(dve, b, u):
            split_lo(dve, UNITS * b + u + RING, u % RING)

        def h_added_tile(b, half, t):
            return (h1_added, BT * b + BT + t + 1) if half else (h0_added, BT * b + t + 1)

        def load_xr(sp, b, half):
            sp.dma_start(xr[:], x[b][:, :, half * HALF:(half + 1) * HALF]).then_inc(xr_in, 16)

        def store_h(sp, b, half):
            for value in (16 * (2 * b + half + 1), 8 * b + 4 * half + 4):
                sp.compute_val(value)
            sp.wait_ge(*h_added_tile(b, half, BT - 1))
            sp.dma_start(h_mid[b][:, :, half * HALF:(half + 1) * HALF], xr[:]).then_inc(h_stored, 16)
            sp.wait_ge(h_stored, 16 * (2 * b + half + 1))
            sp.wait_ge(h_sq, 8 * b + 4 * half + 4)

        def sp_block(sp, b, last):
            for u in range(RING, UNITS):
                p1_retire_load(sp, b, u, last)
                if u == U_K:
                    sp.wait_ge(xt_ready, KT_N * b + KT_N)
                    if last:
                        sp.dma_start(xn[:], h_mid[0]).then_inc(x_in, 16)
                    else:
                        load_x(sp, b + 1)
                if u == UNITS - 2:
                    store_h(sp, b, 0)
                    load_xr(sp, b, 1)
            if last:
                sp.wait_ge(xt_ready, KT_N * b + 2 * KT_N)
                sp.dma_start(xn[:], h_mid[1]).then_inc(h_in[1], 16)
            else:
                for u in range(RING):
                    p1_retire_load(sp, b + 1, u, last)
            store_h(sp, b, 1)
            if not last:
                load_xr(sp, b + 1, 0)

        def pe_block(pe, b, last):
            def unit(u):
                pe.wait_ge(w_lo_ready, UNITS * b + u + 1)

            def feature_quarter(u, bank, c):
                s = u % RING
                for k in (2 * c, 2 * c + 1):
                    w = slice(k * P, (k + 1) * P)
                    ins = three_pass(dense[:, bank, :], w_hi[s][:, w], w_lo[s][:, w],
                                     hn_hi[:, k, :], hn_lo[:, k, :], k == 0, k == KT_N - 1)
                ins.then_inc(dense_done, 1)

            def token_quarter(u, q, t, a_hi, a_lo, cols):
                s = u % RING
                for i in range(2):
                    k = 2 * q + i
                    w = slice(i * HALF, i * HALF + cols)
                    ins = three_pass(dense[:, t, 0:cols], a_hi[:, k, t * P:(t + 1) * P],
                                     a_lo[:, k, t * P:(t + 1) * P], w_hi[s][:, w], w_lo[s][:, w],
                                     k == 0, k == KT_N - 1)
                ins.then_inc(dense_done, 1)

            for q in range(4):
                unit(U_NARROW + q)
                pe.wait_ge(xt_lo, KT_N * b + 2 * q + 2)
                for t in range(BT):
                    if q == 0:
                        pe.wait_ge(h1_added, BT * b + t + 1)
                    token_quarter(U_NARROW + q, q, t, hn_hi, hn_lo, NARROW)

            def rank_transposes():
                pe.wait_ge(narrow_out, BT * b + BT)
                for t in range(BT):
                    ins = nc.tensor.transpose(aux[0:RANK, 0, t * P:(t + 1) * P],
                                              narrow[:, t, N_GLR:N_GLR + RANK], ident)
                ins.then_inc(rank_ready, 1)

            def logits():
                pe.wait_ge(rank_out, b + 1)
                for t in range(BT):
                    ins = nc.tensor.matmul(aux[:, 2 + t // 2, (t % 2) * 256:(t % 2 + 1) * 256],
                                           rank_t[:, t * P:(t + 1) * P], w2[:], start=True, stop=True)
                ins.then_inc(logit_ready, 1)

            def decays():
                pe.wait_ge(la_ready, b + 1)
                for i in range(2):
                    nc.tensor.matmul(aux[:, i, :], tri, gate_b[:, i * HALF:(i + 1) * HALF], start=True, stop=True)
                for t in range(BT):
                    for p in range(2):
                        c = t * 4 + p * 2
                        ins = nc.tensor.matmul(aux[:, 2, c:c + 2], gate_b[:, t * 256 + p * P:t * 256 + (p + 1) * P],
                                               cst[:, C_CHUNK:C_CHUNK + 2], start=True, stop=True)
                ins.then_inc(decay_ready, 1)

            for j in range(5):
                unit(U_Q + j)
                if j < 4:
                    pe.wait_ge(narrow_out, BT * b + j + 1)
                else:
                    pe.wait_ge(q_out, 4 * b + 1)
                for c in range(4):
                    feature_quarter(U_Q + j, j % 4, c)
                if j == 0:
                    rank_transposes()
                if j == 1:
                    logits()
                if j == 3:
                    decays()

            def scores(s):
                t, hs = divmod(s, 2)
                if s == 0:
                    wait_alone(pe, (q_out, 4 * b + 4), (k_out, b + 1), (decay_exp, 2 * b + 2))
                else:
                    wait_alone(pe, (exp_done, 8 * b + s))
                windows = keys[:].rearrange("p c k -> p (c k)")
                for j in range(2):
                    for i in range(2):
                        c = 2 * t + i
                        for g in range(2):
                            r = slice(g * DH, (g + 1) * DH)
                            o = aux[i * CH:(i + 1) * CH, g, j * WIN:(j + 1) * WIN]
                            if c == 0:
                                nc.tensor.matmul(o, row_ind[r, :], mask[r, :], start=True, stop=False)
                            ins = nc.tensor.matmul(o, q_sb[r, 2 * hs + j, c * CH:(c + 1) * CH],
                                                   windows[r, c * PREV:c * PREV + WIN], start=c != 0, stop=True)
                ins.then_inc(scores_ready, 1)

            def prob_transposes(s):
                if s == 0:
                    wait_alone(pe, (exp_done, 8 * b + 1))
                else:
                    wait_alone(pe, (exp_done, 8 * b + s + 1), (swa_out, 8 * b + s))
                for i in range(4):
                    nc.tensor.transpose(aux[0:CH, 2, i * P:(i + 1) * P], probs[:, i, PREV:WIN], ident)
                for i in range(4):
                    ins = nc.tensor.transpose(aux[0:PREV, 3, i * P:(i + 1) * P], probs[:, i, 0:PREV], ident)
                ins.then_inc(pt_ready, 1)

            def weighted_values(s):
                wait_alone(pe, (pt_own_out, 8 * b + s + 1), (pt_prev_out, 8 * b + s + 1))
                for head in range(4):
                    v = slice((head // 2) * DH, (head // 2 + 1) * DH)
                    for own in range(2):
                        for i in range(2):
                            c = 2 * (s // 2) + i
                            q = slice(i * CH, (i + 1) * CH)
                            o = aux[q, 2, head * DH:(head + 1) * DH]
                            if own:
                                ins = nc.tensor.matmul(o, pt_own[:, head, q], values[0:CH, c + 1, v],
                                                       start=False, stop=True)
                            else:
                                nc.tensor.matmul(o, pt_prev[:, head, q], values[:, c, v], start=True, stop=False)
                ins.then_inc(pv_ready, 1)

            def gla_in_piece(c):
                u, r = U_GQ + c // 4, c % 4
                if r == 0:
                    unit(u)
                if u < U_GV:
                    bank = 1 + u - U_GQ
                    if r == 0:
                        pe.wait_ge(q_out, 4 * b + bank + 1)
                    feature_quarter(u, bank, r)
                else:
                    if u == U_GV and r == 0:
                        pe.wait_ge(k_out, b + 1)
                    elif u == U_GV and r < 3:
                        pe.wait_ge(gq_out, 2 * b + r)
                    token_quarter(u, u - U_GV, r, hn_hi, hn_lo, HALF)

            def gg_piece(q, t):
                if t == 0:
                    unit(U_GG + q)
                if q == 0:
                    pe.wait_ge(gv_out, BT * b + t + 1)
                token_quarter(U_GG + q, q, t, hn_hi, hn_lo, HALF)

            gla_in_piece(0)
            scores(0)
            for c in range(1, 3):
                gla_in_piece(c)
            for s in range(7):
                prob_transposes(s)
                scores(s + 1)
                gla_in_piece(3 + 3 * s)
                weighted_values(s)
                gla_in_piece(4 + 3 * s)
                gla_in_piece(5 + 3 * s)
            prob_transposes(7)
            gg_piece(0, 0)
            weighted_values(7)
            for t in range(1, 4):
                gg_piece(0, t)

            wait_alone(pe, (kdec_ready, b + 1), (gv_out, BT * b + BT), (exp_done, 8 * b + 8), (swa_out, 8 * b + 8))
            for c in range(2 * BT):
                t, i = divmod(c, 2)
                r = slice(i * CH, (i + 1) * CH)
                for h in range(GH):
                    j, p = h % 2, h // 2
                    o = (t % 2) * 256 + p * DV
                    ins = nc.tensor.matmul(
                        aux[j * DK:(j + 1) * DK, 2 * i + t // 2, o:o + DV],
                        gate_b[r, t * 256 + h * DK:t * 256 + (h + 1) * DK], gv_sb[r, t, h * DV:(h + 1) * DV],
                        start=True, stop=True)
                if c % 4 == 3:
                    ins.then_inc(u_ready, 1)
            for t in range(BT):
                gg_piece(1, t)

            def gla_read(hf):
                wait_alone(pe, (state_ready, 16 * b + 8 * hf + 8), (gq_out, 2 * b + 2))
                for c in range(4 * hf, 4 * hf + 4):
                    t, i = divmod(c, 2)
                    for h in range(GH):
                        j, p = h % 2, h // 2
                        r = slice(j * DK, (j + 1) * DK)
                        o = (t % 2) * 256 + p * DV
                        ins = nc.tensor.matmul(aux[i * CH:(i + 1) * CH, 2 * j + hf, o:o + DV],
                                               gq_sb[r, p, c * CH:(c + 1) * CH], state[r, c, p, :],
                                               start=True, stop=True)
                ins.then_inc(o_ready, 1)

            gla_read(0)
            for t in range(BT):
                gg_piece(2, t)
            gla_read(1)

            def mix_transposes(k):
                if k < 4:
                    pe.wait_ge(o_out_act, 2 * b + 2)
                    pe.wait_ge(o_out_dve, 2 * b + 2)
                else:
                    pe.wait_ge(gla_out, 2 * b + 2)
                    pe.wait_ge(mt_lo, KT_N * b + k - 3)
                src = mix_swa if k < 4 else gv_sb
                for t in range(BT):
                    ins = nc.tensor.transpose(aux[:, k % 4, t * P:(t + 1) * P],
                                              src[:, t, (k % 4) * P:(k % 4 + 1) * P], ident)
                ins.then_inc(mt_ready, 1)

            def out_unit(half, q, tiles=range(BT)):
                u = U_OUT + 4 * half + q
                unit(u)
                pe.wait_ge(mt_lo, KT_N * b + 2 * q + 2)
                for t in tiles:
                    if q == 0 and half == 0:
                        pe.wait_ge(gg_out, BT * b + t + 1)
                    if q == 0 and half == 1:
                        pe.wait_ge(h0_added, BT * b + t + 1)
                    token_quarter(u, q, t, mix_hi, mix_lo, HALF)

            def next_norm(k0):
                for k in range(k0, k0 + 4):
                    if k < 4:
                        pe.wait_ge(xn_ready, BT * (b + 1) + BT)
                        pe.wait_ge(mt_lo, KT_N * b + 5 + k)
                    else:
                        pe.wait_ge(xt_lo, KT_N * (b + 1) + k - 3)
                    norm1_transpose(pe, b + 1, k)

            gg_piece(3, 0)
            gg_piece(3, 1)
            for k in range(4):
                mix_transposes(k)
            gg_piece(3, 2)
            gg_piece(3, 3)
            out_unit(0, 0)
            out_unit(0, 1, range(0, 2))
            for k in range(4, 8):
                mix_transposes(k)
            out_unit(0, 1, range(2, 4))
            out_unit(0, 2)
            out_unit(0, 3)
            out_unit(1, 0)
            next_norm(0)
            out_unit(1, 1)
            out_unit(1, 2)
            next_norm(4)
            out_unit(1, 3)

        def act_block(act, b, last):
            def retire(u):
                p1_retire_hi(act, b, u)

            def q_evacuate(j):
                act.wait_ge(dense_done, quarter(b, U_Q + j, 3))
                nc.scalar.activation(q_sb[:, j, :], dense[:, j, :], ACT.Copy).then_inc(q_out, 1)

            for u in range(4):
                retire(u)
            q_evacuate(0)
            retire(4)
            act.wait_ge(rank_ready, b + 1)
            nc.scalar.activation(rank_t[0:RANK, :], aux[0:RANK, 0, :], ACT.Copy).then_inc(rank_out, 1)
            q_evacuate(1)
            retire(5)
            act.wait_ge(logit_ready, b + 1)
            nc.scalar.activation(gate_a[:].rearrange("p (a n) -> p a n", a=2), aux[:, 2:4, :],
                                 ACT.Abs).then_inc(gate_act, 1)
            act.wait_ge(gate_act, 3 * b + 1)
            nc.scalar.activation(gate_a[:], gate_a[:], ACT.Exp, scale=-1.0).then_inc(gate_act, 1)
            act.wait_ge(gate_act, 3 * b + 2)
            nc.scalar.activation(gate_a[:], gate_a[:], ACT.Ln, bias=1.0).then_inc(gate_act, 1)
            q_evacuate(2)
            retire(6)
            q_evacuate(3)
            retire(7)
            act.wait_ge(decay_ready, b + 1)
            nc.scalar.activation(gate_a[:].rearrange("p (a n) -> p a n", a=2), aux[:, 0:2, :],
                                 ACT.Exp).then_inc(decay_exp, 1)
            nc.scalar.activation(chunk_g[:], aux[:, 2, 0:4 * BT], ACT.Exp).then_inc(decay_exp, 1)
            retire(8)

            def exps(s):
                act.wait_ge(nmax_ready, 16 * b + 2 * s + 2)
                r = s % 2
                nc.scalar.activation(esink[:, r, :], esink_in[:, r, :], ACT.Exp)
                for i in range(4):
                    ins = nc.scalar.activation(probs[:, i, :], aux[:, i // 2, (i % 2) * WIN:(i % 2 + 1) * WIN],
                                               ACT.Exp, bias=nmax[:, r, i:i + 1], scale=DH ** -0.5,
                                               accum_out=rowsum[:, r, i:i + 1])
                ins.then_inc(exp_done, 1)

            exps(0)
            for s in range(8):
                act.wait_ge(pt_ready, 8 * b + s + 1)
                nc.scalar.activation(pt_own[:].rearrange("p i q -> p (i q)"), aux[0:CH, 2, :],
                                     ACT.Copy).then_inc(pt_own_out, 1)
                if s < 7:
                    exps(s + 1)
                for c in range(3 + 3 * s, 6 + 3 * s):
                    if c >= 24:
                        break
                    if c in (3, 7):
                        i = c // 4
                        act.wait_ge(dense_done, quarter(b, U_GQ + i, 3))
                        nc.scalar.activation(gq_sb[:, i, :], dense[:, 1 + i, :], ACT.Copy,
                                             scale=DK ** -0.5).then_inc(gq_out, 1)
                    if c >= 20:
                        t = c - 20
                        act.wait_ge(dense_done, quarter(b, U_GV + 3, t))
                        nc.scalar.activation(gv_sb[:, t, :], dense[:, t, :], ACT.Copy).then_inc(gv_out, 1)
                    if c % 4 == 3 and c < 23:
                        retire(U_GQ + c // 4)
            retire(U_GG - 1)
            nc.scalar.preload_act_table_set("silu_and_others")
            retire(U_GG)

            def o_evacuate(hf):
                act.wait_ge(o_ready, 2 * b + hf + 1)
                nc.scalar.activation(
                    gv_sb[:, 2 * hf:2 * hf + 2, :].rearrange("p t (a j v) -> p t a j v", a=2, j=2)[:, :, :, 0, :],
                    aux[:, hf, :].rearrange("p (t a v) -> p t a v", t=2, a=2), ACT.Copy).then_inc(o_out_act, 1)
                act.wait_ge(o_out_act, 2 * b + hf + 1)
                act.wait_ge(o_out_dve, 2 * b + hf + 1)
                nc.scalar.activation(q_sb[:, 2 * hf:2 * hf + 2, :], gv_sb[:, 2 * hf:2 * hf + 2, :],
                                     ACT.Square).then_inc(sq_ready, 1)

            retire(U_GG + 1)
            o_evacuate(0)
            retire(U_GG + 2)
            o_evacuate(1)

            def mix_evacuate(k):
                act.wait_ge(mt_ready, KT_N * b + k + 1)
                nc.scalar.activation(mix_hi[:, k, :], aux[:, k % 4, :], ACT.Copy).then_inc(mt_hi, 1)

            def gg_silu(t):
                act.wait_ge(dense_done, quarter(b, U_GG + 3, t))
                nc.scalar.activation(sg[:, t, :], dense[:, t, :], ACT.Silu).then_inc(gg_out, 1)

            gg_silu(0)
            gg_silu(1)
            for k in range(4):
                mix_evacuate(k)
            gg_silu(2)
            gg_silu(3)
            retire(U_GG + 3)
            retire(U_OUT)
            norm1_squares(act, b + 1)
            for k in range(4, 8):
                mix_evacuate(k)
            retire(U_OUT + 1)
            retire(U_OUT + 2)
            retire(U_OUT + 3)

            def h_squares(half):
                for t in range(BT):
                    act.wait_ge(*h_added_tile(b, half, t))
                    nc.scalar.activation(sg[:, t, :], xr[:, t, :], ACT.Square,
                                         accum_out=ssh[:, half, b, t:t + 1]).then_inc(h_sq, 1)
                act.wait_ge(h_sq, 8 * b + 4 * half + 4)

            h_squares(0)
            retire(U_OUT + 4)
            for k in range(4):
                norm1_hi(act, b + 1, k, n2 if last else n1)
            retire(U_OUT + 5)
            retire(U_OUT + 6)
            for k in range(4, 8):
                norm1_hi(act, b + 1, k, n2 if last else n1)
            if not last:
                nc.scalar.preload_act_table_set("natural_log_exp_and_others")
            retire(U_OUT + 7)
            h_squares(1)

        def dve_block(dve, b, last):
            def retire(u):
                p1_retire_lo(dve, b, u)

            nc.vector.tensor_copy(keys[:, 0, 0:CH], keys[:, 2 * BT, 0:CH])
            nc.vector.tensor_copy(values[0:CH, 0, :], values[0:CH, 2 * BT, :]).then_inc(carried, 1)
            for u in range(3):
                retire(u)
            dve.wait_ge(carried, b + 1)
            for t in range(BT):
                dve.wait_ge(dense_done, quarter(b, U_NARROW + 3, t))
                for i in range(2):
                    nc.vector.tensor_copy(values[0:CH, 2 * t + i + 1, :], dense[i * CH:(i + 1) * CH, t, SV:SV + P])
                nc.vector.tensor_copy(narrow[:, t, :], dense[:, t, P:NARROW]).then_inc(narrow_out, 1)
            retire(3)
            retire(4)
            retire(5)
            dve.wait_ge(gate_act, 3 * b + 3)
            nc.vector.scalar_tensor_tensor(out=gate_b[:].rearrange("p (a n) -> p a n", a=2), in0=aux[:, 2:4, :],
                                           scalar=0.0, in1=gate_a[:].rearrange("p (a n) -> p a n", a=2),
                                           op0=ALU.min, op1=ALU.subtract).then_inc(la_ready, 1)
            retire(6)
            retire(7)
            dve.wait_ge(decay_exp, 2 * b + 2)
            nc.vector.tensor_tensor(gate_b[:].rearrange("p (t n) -> p t n", t=BT), narrow[:, :, N_GK:N_GK + GH * DK],
                                    gate_a[:].rearrange("p (t n) -> p t n", t=BT), ALU.mult).then_inc(kdec_ready, 1)
            dve.wait_ge(dense_done, quarter(b, U_K, 3))
            nc.vector.tensor_copy(keys[:, 1:2 * BT + 1, 0:CH],
                                  dense[:, 0, :].rearrange("p (c n) -> p c n", n=CH)).then_inc(k_out, 1)
            retire(8)

            def row_max(s):
                r, hs = s % 2, s % 2
                dve.wait_ge(scores_ready, 8 * b + s + 1)
                nc.vector.tensor_reduce(smax[:, r, :].rearrange("p (g j) -> p g j", g=2),
                                        aux[:, 0:2, 0:2 * WIN].rearrange("p g (j k) -> p g j k", j=2),
                                        AX_X, ALU.max).then_inc(smax_ready, 1)
                dve.wait_ge(smax_ready, 8 * b + s + 1)
                sk = nsink[:, hs * 4:hs * 4 + 4]
                nc.vector.scalar_tensor_tensor(out=nmax[:, r, :], in0=smax[:, r, :], scalar=-(DH ** -0.5), in1=sk,
                                               op0=ALU.mult, op1=ALU.min).then_inc(nmax_ready, 1)
                dve.wait_ge(nmax_ready, 16 * b + 2 * s + 1)
                nc.vector.tensor_tensor(esink_in[:, r, :], nmax[:, r, :], sk, ALU.subtract).then_inc(nmax_ready, 1)

            row_max(0)
            for s in range(8):
                t, hs, r = s // 2, s % 2, s % 2
                if s < 7:
                    dve.wait_ge(pt_ready, 8 * b + s + 1)
                    nc.vector.tensor_copy(pt_prev[:].rearrange("p i q -> p (i q)"), aux[0:PREV, 3, :]).then_inc(pt_prev_out, 1)
                    row_max(s + 1)
                dve.wait_ge(exp_done, 8 * b + s + 1)
                nc.vector.tensor_tensor(denom[:, r, :], rowsum[:, r, :], esink[:, r, :], ALU.add).then_inc(denom_ready, 1)
                dve.wait_ge(denom_ready, 16 * b + 2 * s + 1)
                nc.vector.reciprocal(rden[:, r, :], denom[:, r, :]).then_inc(denom_ready, 1)
                dve.wait_ge(denom_ready, 16 * b + 2 * s + 2)
                dve.wait_ge(pv_ready, 8 * b + s + 1)
                o = mix_swa[:, t, :].rearrange("p (g s j d) -> p g s j d", g=2, s=2, j=2)[:, :, hs, :, :]
                nc.vector.tensor_tensor(o.rearrange("p g j d -> p g j d"),
                                        aux[:, 2, 0:4 * DH].rearrange("p (g j d) -> p g j d", g=2, j=2),
                                        rden[:, r, :].rearrange("p (g j) -> p g j", g=2).unsqueeze(3)
                                        .to_broadcast([P, 2, 2, DH]), ALU.mult).then_inc(swa_out, 1)
                for c in range(3 + 3 * s, 6 + 3 * s):
                    if c < 23 and c % 4 == 3:
                        retire(U_GQ + c // 4)
                if s == 6:
                    dve.wait_ge(pt_ready, 8 * b + 8)
                    nc.vector.tensor_copy(pt_prev[:].rearrange("p i q -> p (i q)"), aux[0:PREV, 3, :]).then_inc(pt_prev_out, 1)
                    retire(U_GG - 1)
            nc.vector.memset(mask[:], 0.0)
            retire(U_GG)

            for c in range(2 * BT):
                t, i = divmod(c, 2)
                if c % 4 == 0:
                    dve.wait_ge(u_ready, 2 * b + c // 4 + 1)
                    dve.wait_ge(decay_exp, 2 * b + 2)
                for p in range(2):
                    if p == 0 and c > 0:
                        dve.wait_ge(state_ready, 16 * b + 2 * c)
                    o = (t % 2) * 256 + p * DV
                    nc.vector.scalar_tensor_tensor(
                        out=state[:, c, p, :], in0=state[:, (c - 1) % (2 * BT), p, :],
                        scalar=chunk_g[:, t * 4 + p * 2 + i:t * 4 + p * 2 + i + 1],
                        in1=aux[:, 2 * i + t // 2, o:o + DV], op0=ALU.mult, op1=ALU.add).then_inc(state_ready, 1)
            retire(U_GG + 1)

            def o_evacuate(hf):
                dve.wait_ge(o_ready, 2 * b + hf + 1)
                nc.vector.tensor_copy(
                    gv_sb[:, 2 * hf:2 * hf + 2, :].rearrange("p t (a j v) -> p t a j v", a=2, j=2)[:, :, :, 1, :],
                    aux[:, 2 + hf, :].rearrange("p (t a v) -> p t a v", t=2, a=2)).then_inc(o_out_dve, 1)

            def o_squares(hf):
                dve.wait_ge(sq_ready, 2 * b + hf + 1)
                nc.vector.tensor_reduce(gss[:, 8 * hf:8 * hf + 8],
                                        q_sb[:, 2 * hf:2 * hf + 2, :].rearrange("p t (h v) -> p (t h) v", h=GH),
                                        AX_X, ALU.add).then_inc(gss_ready, 1)
                dve.wait_ge(gss_ready, 2 * b + hf + 1)
                c = slice(8 * hf, 8 * hf + 8)
                nc.vector.tensor_scalar(gms[:, c], gss[:, c], 1.0 / DV, EPS, ALU.mult, ALU.add).then_inc(gms_ready, 1)

            o_evacuate(0)
            retire(U_GG + 2)
            o_evacuate(1)
            o_squares(0)
            o_squares(1)

            def mix_evacuate(k):
                dve.wait_ge(mt_hi, KT_N * b + k + 1)
                nc.vector.tensor_tensor(mix_lo[:, k, :], aux[:, k % 4, :], mix_hi[:, k, :].bitcast(F32),
                                        ALU.subtract).then_inc(mt_lo, 1)

            for k in range(4):
                mix_evacuate(k)
            retire(U_GG + 3)
            for hf in range(2):
                dve.wait_ge(grs_ready, 2 * b + hf + 1)
                dve.wait_ge(o_out_act, 2 * b + hf + 1)
                v = gv_sb[:, 2 * hf:2 * hf + 2, :].rearrange("p t (h v) -> p (t h) v", h=GH)
                nc.vector.tensor_tensor(v, v, grs[:, 8 * hf:8 * hf + 8].unsqueeze(2).to_broadcast([P, 8, DV]),
                                        ALU.mult).then_inc(gla_scaled, 1)
            for hf in range(2):
                dve.wait_ge(gla_scaled, 2 * b + hf + 1)
                dve.wait_ge(sgw_ready, BT * b + 2 * hf + 2)
                nc.vector.tensor_tensor(gv_sb[:, 2 * hf:2 * hf + 2, :], gv_sb[:, 2 * hf:2 * hf + 2, :],
                                        sg[:, 2 * hf:2 * hf + 2, :], ALU.mult).then_inc(gla_out, 1)
            retire(U_OUT)
            for k in range(4, 8):
                mix_evacuate(k)
            retire(U_OUT + 1)
            norm1_mean(dve, b + 1)
            norm1_scale(dve, b + 1)
            retire(U_OUT + 2)

            def residual(half):
                dve.wait_ge(xr_in, 16 * (2 * b + half + 1))
                for t in range(BT):
                    dve.wait_ge(dense_done, quarter(b, U_OUT + 4 * half + 3, t))
                    nc.vector.tensor_tensor(xr[:, t, :], dense[:, t, :], xr[:, t, :], ALU.add).then_inc(h1_added if half else h0_added, 1)

            residual(0)
            retire(U_OUT + 3)
            retire(U_OUT + 4)
            for k in range(4):
                norm1_lo(dve, b + 1, k, n2 if last else n1)
            retire(U_OUT + 5)
            retire(U_OUT + 6)
            for k in range(4, 8):
                norm1_lo(dve, b + 1, k, n2 if last else n1)
            residual(1)
            retire(U_OUT + 7)

        def pool_block(pool, b, last):
            for hf in range(2):
                c = slice(8 * hf, 8 * hf + 8)
                pool.wait_ge(gms_ready, 2 * b + hf + 1)
                nc.gpsimd.tensor_tensor(grs[:, c], gms[:, c], neg_half[:, c], ALU.pow).then_inc(grs_ready, 1)
            for t in range(BT):
                pool.wait_ge(gg_out, BT * b + t + 1)
                v = sg[:, t, :].rearrange("p (h v) -> p h v", h=GH)
                nc.gpsimd.tensor_tensor(v, v, gwb[:].unsqueeze(1).to_broadcast([P, GH, DV]),
                                        ALU.mult).then_inc(sgw_ready, 1)
            norm1_rstd(pool, b + 1)
            if last:
                pool.wait_ge(h_sq, 8 * b)
                norm2_rstd(pool, 0, (1, 2))

        def run_blocks(eng, program):
            with eng.Fori(0, BLOCKS - 1) as b:
                program(eng, b, False)
            program(eng, BLOCKS - 1, True)

        with nc.Block() as block:
            @block.sync
            def _(sp):
                load_xr(sp, 0, 0)
                for u in range(RING):
                    p1_retire_load(sp, 0, u, False)
                run_blocks(sp, sp_block)

            @block.tensor
            def _(pe):
                run_blocks(pe, pe_block)

            @block.scalar
            def _(act):
                nc.scalar.preload_act_table_set("natural_log_exp_and_others")
                run_blocks(act, act_block)

            @block.vector
            def _(dve):
                nc.vector.memset(rank_t[:], 1.0).then_inc(h1_added, BT)
                run_blocks(dve, dve_block)

            @block.gpsimd
            def _(pool):
                run_blocks(pool, pool_block)
        mixer.close()

        ffn = outer.enter_context(ExitStack())
        ST = 2 * BT
        h = [xn if b == 1 else alloc(ffn, f"h{b}", [P, BT, D]) for b in range(BLOCKS)]
        hs = alloc(ffn, "hs", [P, BT, HALF])
        n2_hi = [hn_hi, alloc(ffn, "n2_hi", [P, KT_N, BLK], F32R)]
        n2_lo = [hn_lo, alloc(ffn, "n2_lo", [P, KT_N, BLK], F32R)]
        a_hi = [alloc(ffn, f"a_hi{i}", [P, 2 * BLK], F32R) for i in range(2)]
        a_lo = [alloc(ffn, f"a_lo{i}", [P, 2 * BLK], F32R) for i in range(2)]
        gate_s = alloc(ffn, "gate_s", [P, 2, BLK])
        a_f = alloc(ffn, "a_f", [P, 2, BLK])
        fwb = alloc(ffn, "fwb", [P, D])
        ssf = alloc(ffn, "ssf", [P, BLOCKS, BT])

        fw_in = sem("fw_in")
        hs_ready = sem("hs_ready")
        ht_ready = sem("ht_ready")
        n2_hi_ready = sem("n2_hi_ready")
        n2_lo_ready = sem("n2_lo_ready")
        silu_done = sem("silu_done")
        mul_done = sem("mul_done")
        act_hi = sem("act_hi")
        act_lo = sem("act_lo")
        h_added = sem("h_added")
        ssf_ready = sem("ssf_ready")
        msf_ready = sem("msf_ready")
        rsf_ready = sem("rsf_ready")
        fin_ready = sem("fin_ready")
        stored = sem("stored")
        GP = 8 + 2 * ST
        ROUND_AFTER = (4, 7, 10, 13)
        ROUNDS = 6

        def round_parts(r):
            block, half = 1 + r // 2, r % 2
            return block, half, block % 2

        def round_scale(eng, scale, r):
            block, half, _ = round_parts(r)
            if half == 0:
                eng.wait_ge(h_in[block], 16)
                eng.wait_ge(rs2_ready, 1 if block < 3 else 2)
            if r > 0:
                eng.wait_ge(ht_ready, 4 * r)
            for t in range(BT):
                ins = scale(hs[:, t, :], h[block][:, t, half * HALF:(half + 1) * HALF], rs2[:, 0, block, t:t + 1])
            ins.then_inc(hs_ready, 1)

        def round_banks(r):
            return dense if r < 2 else aux

        def round_transpose(pe, r):
            pe.wait_ge(hs_ready, r + 1)
            if r == 2:
                pe.wait_ge(silu_done, 4 * GROUPS)
                pe.wait_ge(mul_done, 4 * GROUPS)
            for kk in range(4):
                if r not in (0, 2):
                    pe.wait_ge(n2_lo_ready, 4 * (r - 1) + kk + 1)
                for t in range(BT):
                    ins = nc.tensor.transpose(round_banks(r)[:, kk, t * P:(t + 1) * P],
                                              hs[:, t, kk * P:(kk + 1) * P], ident)
                ins.then_inc(ht_ready, 1)

        def round_hi(act, r):
            _, half, odd = round_parts(r)
            for kk in range(4):
                k = 4 * half + kk
                act.wait_ge(ht_ready, 4 * r + kk + 1)
                nc.scalar.activation(n2_hi[odd][:, k, :], round_banks(r)[:, kk, :], ACT.Copy,
                                     scale=n2[:, k:k + 1]).then_inc(n2_hi_ready, 1)

        def round_lo(dve, r):
            _, half, odd = round_parts(r)
            for kk in range(4):
                k = 4 * half + kk
                dve.wait_ge(n2_hi_ready, 4 * r + kk + 1)
                nc.vector.scalar_tensor_tensor(out=n2_lo[odd][:, k, :], in0=round_banks(r)[:, kk, :],
                                               scalar=n2[:, k:k + 1], in1=n2_hi[odd][:, k, :].bitcast(F32),
                                               op0=ALU.mult, op1=ALU.subtract).then_inc(n2_lo_ready, 1)

        def final_square(act, n):
            b, t = divmod(n, BT)
            act.wait_ge(h_added, 2 * ST * GROUPS * (n // ST + 1) - 2 * ST + 2 * (n % ST) + 2)
            if n > 0:
                act.wait_ge(ssf_ready, n)
            nc.scalar.activation(junk[:], h[b][:, t, :], ACT.Square,
                                 accum_out=ssf[:, b, t:t + 1]).then_inc(ssf_ready, 1)

        def final_mean(dve, n):
            b, t = divmod(n, BT)
            dve.wait_ge(ssf_ready, n + 1)
            nc.vector.tensor_scalar(ms2[:, 1, b, t:t + 1], ssf[:, b, t:t + 1], 1.0 / D, EPS,
                                    ALU.mult, ALU.add).then_inc(msf_ready, 1)

        def final_scale(dve, n):
            b, t = divmod(n, BT)
            dve.wait_ge(rsf_ready, n + 1)
            nc.vector.scalar_tensor_tensor(out=h[b][:, t, :], in0=h[b][:, t, :], scalar=rs2[:, 1, b, t:t + 1],
                                           in1=fwb[:], op0=ALU.mult, op1=ALU.mult).then_inc(fin_ready, 1)

        def final_store(eng, n):
            b, t = divmod(n, BT)
            eng.wait_ge(fin_ready, n + 1)
            eng.dma_start(out[b][:, t, :], h[b][:, t, :]).then_inc(stored, 16)

        def group_pe(pe, sb, g, first=False, last=False):
            G = GROUPS * sb + g
            n = UNITS * BLOCKS + 6 * G

            def piece(fi, th, up):
                u = 2 * fi + up
                s = u % RING
                if th == 0:
                    pe.wait_ge(w_lo_ready, n + u + 1)
                if fi == 1:
                    pe.wait_ge(mul_done if up else silu_done, 4 * G + th + 1)
                if first and sb == 1 and fi == 0 and th == 0:
                    pe.wait_ge(n2_lo_ready, 4 * ROUNDS - 3 + 2 * up)
                for k in range(KT_N):
                    if first and fi == 0 and th == 1 and up == 0:
                        if sb == 0:
                            pe.wait_ge(n2_lo_ready, k + 1)
                        elif k == 0:
                            pe.wait_ge(n2_lo_ready, 4 * ROUNDS)
                    if first and sb == 0 and (fi, th, up) == (0, 0, 1) and k == 4:
                        round_transpose(pe, 0)
                    w = slice(k * P, (k + 1) * P)
                    ins = three_pass(aux[:, 2 * up + th, :], w_hi[s][:, w], w_lo[s][:, w],
                                     n2_hi[th][:, k, :], n2_lo[th][:, k, :], k == 0, k == KT_N - 1)
                ins.then_inc(ffn_done, 1)

            for fi in range(2):
                for th in range(2):
                    for up in range(2):
                        piece(fi, th, up)
                    if first and sb == 0 and fi == 0 and th == 0:
                        round_transpose(pe, 1)
            pe.wait_ge(w_lo_ready, n + 6)
            for o in range(2 * ST):
                tile, nn = divmod(o, 2)
                if o % ST == 0:
                    pe.wait_ge(act_lo, 2 * (2 * G + 1) + o // ST + 1)
                if o > 3:
                    pe.wait_ge(h_added, 2 * ST * G + o - 3)
                for fi in range(2):
                    s = (4 + fi) % RING
                    ins = three_pass(dense[:, o % 4, :], a_hi[fi][:, tile * P:(tile + 1) * P],
                                     a_lo[fi][:, tile * P:(tile + 1) * P], w_hi[s][:, nn * HALF:(nn + 1) * HALF],
                                     w_lo[s][:, nn * HALF:(nn + 1) * HALF], fi == 0, fi == 1)
                ins.then_inc(ffn_done, 1)
                if last and sb == 0 and o in ROUND_AFTER:
                    round_transpose(pe, 2 + ROUND_AFTER.index(o))

        def unit_pieces(u):
            return 4 * (u // 2) + 3 + u % 2 if u < 4 else GP

        def group_act(act, sb, g, first=False, last=False):
            G = GROUPS * sb + g
            final = last and sb == SUPER - 1

            def retire(u):
                if not (final and u >= 3):
                    act.wait_ge(ffn_done, GP * G + unit_pieces(u))
                    split_hi(act, 0, u % RING, (UNITS * BLOCKS) // RING + 2 * G + u // RING + 1)

            for fi in range(2):
                F = 2 * G + fi
                for th in range(2):
                    act.wait_ge(ffn_done, GP * G + 4 * fi + 2 * th + 1)
                    nc.scalar.activation(gate_s[:, th, :], aux[:, th, :], ACT.Silu).then_inc(silu_done, 1)
                    if th == 1:
                        retire(2 * fi)
                    if first and sb == 0 and fi == 0 and th == 0:
                        round_hi(act, 0)
                    act.wait_ge(mul_done, 2 * F + th + 1)
                    nc.scalar.activation(a_hi[fi][:, th * BLK:(th + 1) * BLK], a_f[:, th, :],
                                         ACT.Copy).then_inc(act_hi, 1)
                    if first and sb == 0 and fi == 0 and th == 0:
                        round_hi(act, 1)
                retire(2 * fi + 1)
                if first and sb == 1 and fi == 0:
                    for i in range(ST):
                        final_square(act, i)
            if last and sb == 0:
                round_scale(act, lambda o, i, sc: nc.scalar.activation(o, i, ACT.Copy, scale=sc), 2)
                for r in range(2, ROUNDS):
                    round_hi(act, r)
                    if r < ROUNDS - 1:
                        round_scale(act, lambda o, i, sc: nc.scalar.activation(o, i, ACT.Copy, scale=sc), r + 1)
            retire(4)
            retire(5)
            if final:
                for i in range(ST, 2 * ST):
                    final_square(act, i)

        def group_dve(dve, sb, g, first=False, last=False):
            G = GROUPS * sb + g
            n = UNITS * BLOCKS + 6 * G
            final = last and sb == SUPER - 1

            def retire(u):
                if not (final and u >= 3):
                    split_lo(dve, n + u + RING, u % RING)

            def block1_scale(r):
                round_scale(dve, lambda o, i, sc: nc.vector.tensor_scalar(o, i, sc, None, ALU.mult), r)

            if first and sb == 0:
                block1_scale(0)
                block1_scale(1)
                round_lo(dve, 0)
            for fi in range(2):
                F = 2 * G + fi
                for th in range(2):
                    m = slice(th * BLK, (th + 1) * BLK)
                    if th == 1:
                        retire(2 * fi)
                    dve.wait_ge(ffn_done, GP * G + 4 * fi + 2 * th + 2)
                    dve.wait_ge(silu_done, 2 * F + th + 1)
                    nc.vector.tensor_tensor(a_f[:, th, :], aux[:, 2 + th, :], gate_s[:, th, :],
                                            ALU.mult).then_inc(mul_done, 1)
                    dve.wait_ge(act_hi, 2 * F + th + 1)
                    nc.vector.tensor_tensor(a_lo[fi][:, m], a_f[:, th, :], a_hi[fi][:, m].bitcast(F32),
                                            ALU.subtract).then_inc(act_lo, 1)
                    if first and sb == 0 and fi == 0 and th == 0:
                        round_lo(dve, 1)
                    if first and sb == 1 and fi == 1 and th == 0:
                        for i in (3, 4):
                            final_scale(dve, i)
                retire(2 * fi + 1)
                if first and sb == 1 and fi == 0:
                    dve.wait_ge(fw_in, 16)
                    for i in range(ST):
                        final_mean(dve, i)
                    for i in range(3):
                        final_scale(dve, i)
            for o in range(2 * ST):
                tile, nn = divmod(o, 2)
                bb, t = divmod(tile, BT)
                dve.wait_ge(ffn_done, GP * G + 8 + o + 1)
                dst = h[2 * sb + bb][:, t, nn * HALF:(nn + 1) * HALF]
                if first and sb == 0 and o in (0, ST):
                    dve.wait_ge(h_in[bb], 16)
                nc.vector.tensor_tensor(dst, dense[:, o % 4, :], dst, ALU.add).then_inc(h_added, 1)
                if last and sb == 0 and o - 1 in ROUND_AFTER:
                    round_lo(dve, 2 + ROUND_AFTER.index(o - 1))
                if first and sb == 1 and o in (5, 8, 11):
                    final_scale(dve, o // 3 + 4)
                if final and nn == 1:
                    if tile > 0:
                        final_mean(dve, ST + tile - 1)
                    if tile > 1:
                        final_scale(dve, ST + tile - 2)
            if final:
                final_mean(dve, 2 * ST - 1)
                final_scale(dve, 2 * ST - 2)
                final_scale(dve, 2 * ST - 1)
            retire(4)
            retire(5)

        def group_sp(sp, sb, g, first=False, last=False):
            G = GROUPS * sb + g
            for u in range(6):
                if last and sb == SUPER - 1 and u >= 3:
                    break
                sp.wait_ge(w_lo_ready, UNITS * BLOCKS + 6 * G + u + 1)
                load_unit(sp, u % RING, w_ffn[u - 3] if last and u >= 3 else w_ffn[6 * g + u + RING])
            if first and sb == 1:
                for n in range(ST):
                    final_store(sp, n)
            if last and sb == 1:
                for n in range(ST, 2 * ST):
                    final_store(sp, n)

        def run_groups(eng, program):
            for sb in range(SUPER):
                program(eng, sb, 0, first=True)
                with eng.Fori(1, GROUPS - 1) as g:
                    program(eng, sb, g)
                program(eng, sb, GROUPS - 1, last=True)

        with nc.Block() as block:
            @block.sync
            def _(sp):
                sp.dma_start(h[0][:], h_mid[0]).then_inc(h_in[0], 16)
                sp.dma_start(fwb[:], fw).then_inc(fw_in, 16)
                run_groups(sp, group_sp)
                sp.wait_ge(stored, 16 * 2 * ST)

            @block.tensor
            def _(pe):
                run_groups(pe, group_pe)

            @block.scalar
            def _(act):
                nc.scalar.preload_act_table_set("silu_and_others")
                run_groups(act, group_act)

            @block.gpsimd
            def _(pool):
                norm2_rstd(pool, 1, (3,))
                pool.wait_ge(ffn_done, 8)
                for b in (2, 3):
                    pool.dma_start(h[b][:], h_mid[b]).then_inc(h_in[b], 16)
                for n in range(2 * ST):
                    b, t = divmod(n, BT)
                    pool.wait_ge(msf_ready, n + 1)
                    nc.gpsimd.tensor_tensor(rs2[:, 1, b, t:t + 1], ms2[:, 1, b, t:t + 1], neg_half[:, 0:1],
                                            ALU.pow).then_inc(rsf_ready, 1)

            @block.vector
            def _(dve):
                run_groups(dve, group_dve)
        ffn.close()


def pack(w, rows, cols):
    import numpy as np
    k = w.shape[0] // P
    return np.ascontiguousarray(w.reshape(k // rows, rows, P, cols).transpose(0, 2, 1, 3)).reshape(k // rows, P, -1)


def kernel(x, meta_tokens, norm1_w, w_in, gla_gate_w2, gla_gate_b, gla_norm_w, swa_sinks, w_out,
           norm2_w, w_gate, w_up, w_down, final_norm_w):
    import numpy as np
    import concourse.bacc as bacc
    from concourse.bass_utils import run_bass_kernel_spmd

    w_in, w_out = np.asarray(w_in)[0], np.asarray(w_out)[0]
    w_gate, w_up, w_down = np.asarray(w_gate)[0], np.asarray(w_up)[0], np.asarray(w_down)[0]
    narrow = np.zeros((D, HALF), w_in.dtype)
    narrow[:, SV:SV + P] = w_in[:, 640:768]
    narrow[:, GK:GK + 256] = w_in[:, 1024:1280]
    narrow[:, GLR:GLR + RANK] = w_in[:, 2304:2320]
    units = [pack(narrow, 2, HALF)]
    for j in range(4):
        pair = np.concatenate([w_in[:, j * DH:(j + 1) * DH], w_in[:, (4 + j) * DH:(5 + j) * DH]], axis=1)
        units.append(pack(pair, 8, P))
    units.append(pack(w_in[:, 512:640], 8, P))
    for j in range(2):
        units.append(pack(w_in[:, 768 + j * P:768 + (j + 1) * P], 8, P))
    units += [pack(w_in[:, 1280:1792], 2, HALF), pack(w_in[:, 1792:2304], 2, HALF)]
    units += [pack(w_out[:, 0:HALF], 2, HALF), pack(w_out[:, HALF:D], 2, HALF)]
    w_block = np.concatenate(units)
    units = []
    for g in range(GROUPS):
        for f in (2 * g, 2 * g + 1):
            for w in (w_gate, w_up):
                units.append(pack(w[:, f * P:(f + 1) * P], 8, P))
        units.append(w_down[2 * g * P:2 * (g + 1) * P].reshape(2, P, D))
    w_ffn = np.concatenate(units)

    consts = np.zeros((P, CONSTS), np.float32)
    masks = np.zeros((P, MASKS), np.float32)
    i = np.arange(P)
    consts[:, C_ID:C_ID + P] = np.eye(P)
    same = i[:, None] // CH == i[None, :] // CH
    consts[:, C_TRI:C_TRI + P] = np.where(same & (i[:, None] > i[None, :]), 1 / 16, 0)
    for c in range(2):
        consts[c * CH:(c + 1) * CH, C_CHUNK + c] = 1 / 16
    for r in (0, DH):
        masks[r, M_ROW:M_ROW + CH] = 1
        masks[r, M_MASK:M_MASK + CH] = -1e30

    def tiles(w):
        return np.ascontiguousarray(np.asarray(w).reshape(KT_N, P).T)

    def rows(w):
        w = np.asarray(w).reshape(1, -1)
        return np.ascontiguousarray(np.broadcast_to(w, (P, w.shape[1])))

    arrays = {
        "x": np.ascontiguousarray(np.asarray(x)).reshape(BLOCKS, BT, P, D),
        "meta": np.ascontiguousarray(meta_tokens),
        "n1w": tiles(norm1_w), "n2w": tiles(norm2_w), "fw": rows(final_norm_w),
        "w_block": w_block, "w_ffn": w_ffn,
        "w2b": np.concatenate([np.asarray(gla_gate_w2)[0], np.asarray(gla_gate_b).reshape(1, -1)]),
        "gw": rows(gla_norm_w), "sinks": rows(swa_sinks), "consts": consts, "masks": masks,
    }
    nc = bacc.Bacc("TRN2", target_bir_lowering=False, num_devices=1)
    args = {n: nc.dram_tensor(f"in_{n}", a.shape, F32, kind="ExternalInput").ap() for n, a in arrays.items()}
    h_mid = nc.dram_tensor("h_mid", (BLOCKS, P, BT, D), F32).ap()
    out = nc.dram_tensor("out_0", (BLOCKS, BT, P, D), F32, kind="ExternalOutput").ap()
    args["x"] = args["x"].rearrange("b t p d -> b p t d")
    build(nc, h_mid=h_mid, out=out.rearrange("b t p d -> b p t d"), **args)
    r = run_bass_kernel_spmd(nc, [{f"in_{n}": a for n, a in arrays.items()}], core_ids=[0])
    return r.results[0]["out_0"].reshape(1, BLOCKS * BLK, D)
```
